# Optimizing a Trainium2 kernel written in Bass

```python
import math
import jax, jax.numpy as jnp
from jax import lax
import numpy as np

D_MODEL = 1024
BATCH = 1
SEQ = 256
DEPTH = 1

CHUNK = 64
Q_BLOCK = 128

MIX_WIDTH = D_MODEL
HG_WIDTH = MIX_WIDTH // 2
HG_HEADS = 4
HG_DK = HG_WIDTH // HG_HEADS
FOX_WIDTH = MIX_WIDTH - HG_WIDTH
FOX_HEADS = 8
FOX_DH = FOX_WIDTH // FOX_HEADS
IN_COLS = 4 * HG_WIDTH + 3 * FOX_WIDTH + FOX_HEADS
N_EXPERT_GROUPS = 4
EXPERTS_PER_GROUP = 4
N_EXPERTS = N_EXPERT_GROUPS * EXPERTS_PER_GROUP
TOP_K = 2
EXPERT_HIDDEN = D_MODEL // 2
NORM_EPS = 1e-6
NEG_INF = -1e30


def rms_norm(x, gain):
    xf = x.astype(jnp.float32)
    y = xf * lax.rsqrt(jnp.mean(xf * xf, axis=-1, keepdims=True) + NORM_EPS)
    return (y * gain.astype(jnp.float32)).astype(x.dtype)

def hgrn2_mixer(q_raw, f_raw, i_raw, g_raw, lower_bound, norm_gain):
    B, S, _ = q_raw.shape
    nc = S // CHUNK
    f32 = jnp.float32
    q = jax.nn.silu(q_raw.astype(f32))
    lb = lower_bound.astype(f32)
    f = lb + (1.0 - lb) * jax.nn.sigmoid(f_raw.astype(f32))
    log_f = jnp.log(f)
    k = 1.0 - f
    v = i_raw.astype(f32)

    def to_chunks(t):
        return t.reshape(B, nc, CHUNK, HG_HEADS, HG_DK).transpose(1, 0, 3, 2, 4)

    causal = jnp.tril(jnp.ones((CHUNK, CHUNK), dtype=bool))

    def step(state, inp):
        qc, kc, vc, lfc = inp
        b = jnp.cumsum(lfc, axis=2)
        o_inter = jnp.einsum('bhtk,bhkv->bhtv', qc * jnp.exp(b), state)
        diff = b[:, :, :, None, :] - b[:, :, None, :, :]
        decay = jnp.where(causal[:, :, None], jnp.exp(jnp.minimum(diff, 0.0)), 0.0)
        scores = jnp.einsum('bhtk,bhtsk,bhsk->bhts', qc, decay, kc)
        o_intra = jnp.einsum('bhts,bhsv->bhtv', scores, vc)
        b_last = b[:, :, -1:, :]
        new_state = (jnp.exp(b_last[:, :, 0, :])[..., None] * state
                     + jnp.einsum('bhsk,bhsv->bhkv', kc * jnp.exp(b_last - b), vc))
        return new_state, o_inter + o_intra

    s0 = jnp.zeros((B, HG_HEADS, HG_DK, HG_DK), f32)
    _, o = lax.scan(step, s0, (to_chunks(q), to_chunks(k), to_chunks(v), to_chunks(log_f)))
    o = o.transpose(1, 0, 3, 2, 4).reshape(B, S, HG_HEADS, HG_DK)
    o = rms_norm(o, norm_gain)
    o = o.reshape(B, S, HG_WIDTH) * jax.nn.silu(g_raw.astype(f32))
    return o.astype(q_raw.dtype)

def fox_mixer(q_raw, k_raw, v_raw, f_raw, f_bias, norm_gain):
    B, S, _ = q_raw.shape
    f32 = jnp.float32

    def heads(t):
        return t.astype(f32).reshape(B, S, FOX_HEADS, FOX_DH).transpose(0, 2, 1, 3)

    q = heads(q_raw) * (FOX_DH ** -0.5)
    k = heads(k_raw)
    v = heads(v_raw)
    log_f = jax.nn.log_sigmoid(f_raw.astype(f32) + f_bias.astype(f32))
    cum = jnp.cumsum(log_f, axis=1).transpose(0, 2, 1)
    key_pos = jnp.arange(S)

    def block(i):
        start = i * Q_BLOCK
        qb = lax.dynamic_slice_in_dim(q, start, Q_BLOCK, axis=2)
        cb = lax.dynamic_slice_in_dim(cum, start, Q_BLOCK, axis=2)
        logits = jnp.einsum('bhtd,bhsd->bhts', qb, k) + (cb[..., :, None] - cum[..., None, :])
        mask = (start + jnp.arange(Q_BLOCK))[:, None] >= key_pos[None, :]
        logits = jnp.where(mask, logits, NEG_INF)
        p = jax.nn.softmax(logits, axis=-1)
        return jnp.einsum('bhts,bhsd->bhtd', p, v)

    o = lax.map(block, jnp.arange(S // Q_BLOCK))
    o = o.transpose(1, 0, 3, 2, 4).reshape(B, S, FOX_HEADS, FOX_DH)
    o = rms_norm(o, norm_gain)
    return o.reshape(B, S, FOX_WIDTH).astype(q_raw.dtype)

def hier_moe(x, w_group, b_group, w_expert, b_expert, w_gate, w_up, w_down):
    B, S, D = x.shape
    t = x.reshape(-1, D)
    pg = jax.nn.softmax((t @ w_group + b_group).astype(jnp.float32), axis=-1)
    gsel = jnp.argmax(pg, axis=-1)
    pg_sel = jnp.max(pg, axis=-1)
    e_logits = (t @ w_expert + b_expert).astype(jnp.float32).reshape(-1, N_EXPERT_GROUPS, EXPERTS_PER_GROUP)
    e_logits = jnp.take_along_axis(e_logits, gsel[:, None, None], axis=1)[:, 0]
    pe = jax.nn.softmax(e_logits, axis=-1)
    top_p, top_i = lax.top_k(pe, TOP_K)
    top_p = top_p / jnp.sum(top_p, axis=-1, keepdims=True)
    expert_id = gsel[:, None] * EXPERTS_PER_GROUP + top_i
    weights = pg_sel[:, None] * top_p
    gates = jnp.sum(jax.nn.one_hot(expert_id, N_EXPERTS, dtype=jnp.float32) * weights[..., None], axis=1)
    gates = gates.astype(t.dtype)
    y = jnp.zeros_like(t)
    for e in range(N_EXPERTS):
        h = jax.nn.silu(t @ w_gate[e]) * (t @ w_up[e])
        y = y + gates[:, e:e + 1] * (h @ w_down[e])
    return y.reshape(B, S, D)

def first_inputs(seed: int = 0) -> dict:
    key = jax.random.key(seed)
    ks = jax.random.split(key, 20)
    f32 = jnp.float32
    L, D = DEPTH, D_MODEL
    nrm = lambda k, shape, scale: jax.random.normal(k, shape, f32) * scale
    return {
        "x": jax.random.normal(ks[0], (BATCH, SEQ, D), f32),
        "attn_norm": 1.0 + nrm(ks[1], (L, D), 0.02),
        "w_in": nrm(ks[2], (L, D, IN_COLS), D ** -0.5),
        "hg_lb_logits": nrm(ks[3], (L + 1, HG_WIDTH), 0.5),
        "hg_norm": 1.0 + nrm(ks[4], (L, HG_DK), 0.02),
        "fox_f_bias": nrm(ks[5], (L, FOX_HEADS), 0.1),
        "fox_norm": 1.0 + nrm(ks[6], (L, FOX_DH), 0.02),
        "w_out": nrm(ks[7], (L, MIX_WIDTH, D), MIX_WIDTH ** -0.5),
        "ffn_norm": 1.0 + nrm(ks[8], (L, D), 0.02),
        "w_group": nrm(ks[9], (L, D, N_EXPERT_GROUPS), D ** -0.5),
        "b_group": nrm(ks[10], (L, N_EXPERT_GROUPS), 0.01),
        "w_expert": nrm(ks[11], (L, D, N_EXPERTS), D ** -0.5),
        "b_expert": nrm(ks[12], (L, N_EXPERTS), 0.01),
        "w_gate": nrm(ks[13], (L, N_EXPERTS, D, EXPERT_HIDDEN), D ** -0.5),
        "w_up": nrm(ks[14], (L, N_EXPERTS, D, EXPERT_HIDDEN), D ** -0.5),
        "w_down": nrm(ks[15], (L, N_EXPERTS, EXPERT_HIDDEN, D), EXPERT_HIDDEN ** -0.5),
        "final_norm": 1.0 + nrm(ks[16], (D,), 0.02),
    }

def first_block(x, attn_norm, w_in, hg_lb_logits, hg_norm, fox_f_bias, fox_norm, w_out, ffn_norm,
              w_group, b_group, w_expert, b_expert, w_gate, w_up, w_down, final_norm):
    lb_all = jnp.cumsum(jax.nn.softmax(hg_lb_logits.astype(jnp.float32), axis=0), axis=0)
    o0 = 0
    o1 = o0 + HG_WIDTH
    o2 = o1 + HG_WIDTH
    o3 = o2 + HG_WIDTH
    o4 = o3 + HG_WIDTH
    o5 = o4 + FOX_WIDTH
    o6 = o5 + FOX_WIDTH
    o7 = o6 + FOX_WIDTH
    h = x
    for l in range(DEPTH):
        xn = rms_norm(h, attn_norm[l])
        u = xn @ w_in[l]
        o_a = hgrn2_mixer(u[..., o0:o1], u[..., o1:o2], u[..., o2:o3], u[..., o3:o4],
                          lb_all[l], hg_norm[l])
        o_b = fox_mixer(u[..., o4:o5], u[..., o5:o6], u[..., o6:o7], u[..., o7:IN_COLS],
                        fox_f_bias[l], fox_norm[l])
        h = h + jnp.concatenate([o_a, o_b], axis=-1) @ w_out[l]
        h = h + hier_moe(rms_norm(h, ffn_norm[l]), w_group[l], b_group[l], w_expert[l], b_expert[l],
                         w_gate[l], w_up[l], w_down[l])
    return rms_norm(h, final_norm)


DEPTH_2 = 2

RMS_EPS = 1e-6
D_FF = 2816

SSD_WIDTH = D_MODEL
SSD_HEADDIM = 64
SSD_HEADS = SSD_WIDTH // SSD_HEADDIM
SSD_GROUPS = 2
SSD_HPG = SSD_HEADS // SSD_GROUPS
SSD_STATE = 128
SSD_CONV = 5
SSD_CHUNK = 128
SSD_XBC = SSD_WIDTH + 2 * SSD_GROUPS * SSD_STATE

MLA_HEADS = 8
MLA_Q_LORA = D_MODEL // 4
MLA_KV_LORA = D_MODEL // 8
MLA_NOPE = 64
MLA_ROPE = 32
MLA_QK = MLA_NOPE + MLA_ROPE
MLA_V = 64
MLA_WIDTH = MLA_HEADS * MLA_V
ROPE_BASE = 10000.0
ATTN_BLOCK = 128

CONV_WIDTH = D_MODEL // 2
CONV_GROUPS = 8
CONV_K = 3

D_MIX = SSD_WIDTH + MLA_WIDTH + CONV_WIDTH
IN_SIZES = (SSD_WIDTH, SSD_XBC, 2 * SSD_HEADS, MLA_Q_LORA, MLA_KV_LORA, MLA_ROPE, CONV_WIDTH, CONV_WIDTH, CONV_WIDTH)
D_IN = SSD_WIDTH + SSD_XBC + 2 * SSD_HEADS + MLA_Q_LORA + MLA_KV_LORA + MLA_ROPE + 3 * CONV_WIDTH


def rms_norm_2(x, g):
    xf = x.astype(jnp.float32)
    y = xf * lax.rsqrt(jnp.mean(xf * xf, axis=-1, keepdims=True) + RMS_EPS)
    return (y * g.astype(jnp.float32)).astype(x.dtype)

def group_rms_norm(x, g, n_groups):
    shp = x.shape
    xg = x.reshape(shp[:-1] + (n_groups, shp[-1] // n_groups))
    return rms_norm_2(xg, g.reshape(n_groups, -1)).reshape(shp)

def swiglu(x, w_gate, w_up, w_down):
    return (jax.nn.silu(x @ w_gate) * (x @ w_up)) @ w_down

def depthwise_conv(x, w):
    k, c = w.shape
    return lax.conv_general_dilated(x, w[:, None, :].astype(x.dtype), window_strides=(1,),
                                    padding=[(k // 2, k // 2)],
                                    dimension_numbers=('NWC', 'WIO', 'NWC'),
                                    feature_group_count=c)

def rope(x, pos):
    half = x.shape[-1] // 2
    inv = ROPE_BASE ** (-jnp.arange(half, dtype=jnp.float32) / half)
    ang = pos.astype(jnp.float32)[..., None] * inv
    cos = jnp.cos(ang)[:, :, None, :]
    sin = jnp.sin(ang)[:, :, None, :]
    xf = x.astype(jnp.float32)
    x1, x2 = xf[..., :half], xf[..., half:]
    return jnp.concatenate([x1 * cos - x2 * sin, x1 * sin + x2 * cos], axis=-1).astype(x.dtype)

def split_points(sizes):
    pts, acc = [], 0
    for n in sizes[:-1]:
        acc += n
        pts.append(acc)
    return pts

def ssd_chunked(x, dt, a, bm, cm):
    bsz, s = x.shape[0], x.shape[1]
    nc, L = s // SSD_CHUNK, SSD_CHUNK
    xc = x.reshape(bsz, nc, L, SSD_GROUPS, SSD_HPG, SSD_HEADDIM)
    dtc = dt.reshape(bsz, nc, L, SSD_GROUPS, SSD_HPG)
    bc = bm.reshape(bsz, nc, L, SSD_GROUPS, SSD_STATE)
    cc = cm.reshape(bsz, nc, L, SSD_GROUPS, SSD_STATE)
    xd = xc * dtc[..., None]
    a_cs = jnp.cumsum(dtc * a, axis=2)
    seg = a_cs[:, :, :, None] - a_cs[:, :, None, :]
    lower = jnp.tril(jnp.ones((L, L), dtype=bool))[None, None, :, :, None, None]
    decay = jnp.exp(jnp.where(lower, seg, -jnp.inf))
    cb = jnp.einsum('bclgn,bcsgn->bclsg', cc, bc)
    y_diag = jnp.einsum('bclsg,bclsgr,bcsgrp->bclgrp', cb, decay, xd)
    decay_states = jnp.exp(a_cs[:, :, -1:] - a_cs)
    states = jnp.einsum('bclgn,bclgr,bclgrp->bcgrpn', bc, decay_states, xd)
    chunk_decay = jnp.exp(a_cs[:, :, -1])

    def step(carry, inp):
        st, dec = inp
        return carry * dec[..., None, None] + st, carry

    init = jnp.zeros_like(states[:, 0])
    _, prev = lax.scan(step, init, (jnp.moveaxis(states, 1, 0), jnp.moveaxis(chunk_decay, 1, 0)))
    prev = jnp.moveaxis(prev, 0, 1)
    y_off = jnp.einsum('bclgn,bcgrpn,bclgr->bclgrp', cc, prev, jnp.exp(a_cs))
    return (y_diag + y_off).reshape(bsz, s, SSD_GROUPS, SSD_HPG, SSD_HEADDIM)

def ssd_mixer(z, xbc, dt_raw, conv_w, conv_b, dt_bias, a_log, d_skip, norm_g):
    bsz, s = z.shape[0], z.shape[1]
    xbc = jax.nn.silu(depthwise_conv(xbc, conv_w) + conv_b)
    xs = xbc[..., :SSD_WIDTH].reshape(bsz, s, SSD_GROUPS, SSD_HPG, SSD_HEADDIM).astype(jnp.float32)
    bm = xbc[..., SSD_WIDTH:SSD_WIDTH + SSD_GROUPS * SSD_STATE].reshape(bsz, s, SSD_GROUPS, SSD_STATE).astype(jnp.float32)
    cm = xbc[..., SSD_WIDTH + SSD_GROUPS * SSD_STATE:].reshape(bsz, s, SSD_GROUPS, SSD_STATE).astype(jnp.float32)
    dt = jax.nn.softplus(dt_raw.astype(jnp.float32).reshape(bsz, s, 2, SSD_GROUPS, SSD_HPG)
                         + dt_bias.astype(jnp.float32).reshape(2, SSD_GROUPS, SSD_HPG))
    a = -jnp.exp(a_log.astype(jnp.float32)).reshape(2, SSD_GROUPS, SSD_HPG)
    y_fwd = ssd_chunked(xs, dt[:, :, 0], a[0], bm, cm)
    y_bwd = jnp.flip(ssd_chunked(jnp.flip(xs, 1), jnp.flip(dt[:, :, 1], 1), a[1],
                                 jnp.flip(bm, 1), jnp.flip(cm, 1)), 1)
    y = y_fwd + y_bwd + xs * d_skip.astype(jnp.float32).reshape(SSD_GROUPS, SSD_HPG)[..., None]
    y = y.reshape(bsz, s, SSD_WIDTH) * jax.nn.silu(z.astype(jnp.float32))
    return group_rms_norm(y, norm_g, SSD_GROUPS).astype(z.dtype)

def mla_mixer(q_lat, kv_lat, k_pe, positions, q_norm, w_uq, kv_norm, w_ukv,
              q_head_norm, k_head_norm, out_norm):
    bsz, s = q_lat.shape[0], q_lat.shape[1]
    q = (rms_norm_2(q_lat, q_norm) @ w_uq).reshape(bsz, s, MLA_HEADS, MLA_QK)
    kv = (rms_norm_2(kv_lat, kv_norm) @ w_ukv).reshape(bsz, s, MLA_HEADS, MLA_NOPE + MLA_V)
    k_nope, v = kv[..., :MLA_NOPE], kv[..., MLA_NOPE:]
    k = jnp.concatenate([k_nope, jnp.broadcast_to(k_pe[:, :, None, :], (bsz, s, MLA_HEADS, MLA_ROPE))], axis=-1)
    q = rms_norm_2(q, q_head_norm)
    k = rms_norm_2(k, k_head_norm)
    q = jnp.concatenate([q[..., :MLA_NOPE], rope(q[..., MLA_NOPE:], positions)], axis=-1)
    k = jnp.concatenate([k[..., :MLA_NOPE], rope(k[..., MLA_NOPE:], positions)], axis=-1)
    scale = MLA_QK ** -0.5
    nb = s // ATTN_BLOCK
    q_blocks = q.reshape(bsz, nb, ATTN_BLOCK, MLA_HEADS, MLA_QK).swapaxes(0, 1)

    def attend(qb):
        sc = jnp.einsum('bqhd,bkhd->bhqk', qb, k).astype(jnp.float32) * scale
        p = jax.nn.softmax(sc, axis=-1).astype(v.dtype)
        return jnp.einsum('bhqk,bkhd->bqhd', p, v)

    o = lax.map(attend, q_blocks).swapaxes(0, 1).reshape(bsz, s, MLA_HEADS, MLA_V)
    return rms_norm_2(o, out_norm.reshape(MLA_HEADS, MLA_V)).reshape(bsz, s, MLA_WIDTH)

def conv_mixer(h_in, b_gate, c_gate, conv_w, out_norm):
    y = b_gate * depthwise_conv(c_gate * h_in, conv_w)
    return group_rms_norm(y, out_norm, CONV_GROUPS)

def second_inputs(seed: int = 0) -> dict:
    key = jax.random.key(seed)
    k = jax.random.split(key, 32)
    f32 = jnp.float32

    def w(i, shape, fan_in):
        return jax.random.normal(k[i], shape, f32) * (fan_in ** -0.5)

    def gain(i, shape):
        return 1.0 + 0.05 * jax.random.normal(k[i], shape, f32)

    u = jax.random.uniform(k[9], (DEPTH_2, 2, SSD_HEADS), f32)
    dt0 = jnp.exp(u * (math.log(0.1) - math.log(1e-3)) + math.log(1e-3))
    ssd_dt_bias = dt0 + jnp.log(-jnp.expm1(-dt0))
    ssd_a_log = jnp.log(jax.random.uniform(k[10], (DEPTH_2, 2, SSD_HEADS), f32, 1.0, 16.0))
    positions = jnp.broadcast_to(jnp.arange(SEQ, dtype=jnp.int32)[None, :], (BATCH, SEQ))
    return {
        'x': jax.random.normal(k[0], (BATCH, SEQ, D_MODEL), f32),
        'positions': positions,
        'ffn1_norm': gain(1, (DEPTH_2, D_MODEL)),
        'ffn1_w_gate': w(2, (DEPTH_2, D_MODEL, D_FF), D_MODEL),
        'ffn1_w_up': w(3, (DEPTH_2, D_MODEL, D_FF), D_MODEL),
        'ffn1_w_down': w(4, (DEPTH_2, D_FF, D_MODEL), D_FF),
        'mix_norm': gain(5, (DEPTH_2, D_MODEL)),
        'w_in': w(6, (DEPTH_2, D_MODEL, D_IN), D_MODEL),
        'ssd_conv_w': w(7, (DEPTH_2, SSD_CONV, SSD_XBC), SSD_CONV),
        'ssd_conv_b': 0.02 * jax.random.normal(k[8], (DEPTH_2, SSD_XBC), f32),
        'ssd_dt_bias': ssd_dt_bias,
        'ssd_a_log': ssd_a_log,
        'ssd_d': 1.0 + 0.1 * jax.random.normal(k[11], (DEPTH_2, SSD_HEADS), f32),
        'ssd_norm': gain(12, (DEPTH_2, SSD_WIDTH)),
        'mla_q_norm': gain(13, (DEPTH_2, MLA_Q_LORA)),
        'mla_w_uq': w(14, (DEPTH_2, MLA_Q_LORA, MLA_HEADS * MLA_QK), MLA_Q_LORA),
        'mla_kv_norm': gain(15, (DEPTH_2, MLA_KV_LORA)),
        'mla_w_ukv': w(16, (DEPTH_2, MLA_KV_LORA, MLA_HEADS * (MLA_NOPE + MLA_V)), MLA_KV_LORA),
        'mla_q_head_norm': gain(17, (DEPTH_2, MLA_QK)),
        'mla_k_head_norm': gain(18, (DEPTH_2, MLA_QK)),
        'mla_out_norm': gain(19, (DEPTH_2, MLA_WIDTH)),
        'conv_w': w(20, (DEPTH_2, CONV_K, CONV_WIDTH), CONV_K),
        'conv_out_norm': gain(21, (DEPTH_2, CONV_WIDTH)),
        'w_out': w(22, (DEPTH_2, D_MIX, D_MODEL), D_MIX),
        'ffn2_norm': gain(23, (DEPTH_2, D_MODEL)),
        'ffn2_w_gate': w(24, (DEPTH_2, D_MODEL, D_FF), D_MODEL),
        'ffn2_w_up': w(25, (DEPTH_2, D_MODEL, D_FF), D_MODEL),
        'ffn2_w_down': w(26, (DEPTH_2, D_FF, D_MODEL), D_FF),
    }

def second_block(x, positions, ffn1_norm, ffn1_w_gate, ffn1_w_up, ffn1_w_down, mix_norm, w_in,
              ssd_conv_w, ssd_conv_b, ssd_dt_bias, ssd_a_log, ssd_d, ssd_norm,
              mla_q_norm, mla_w_uq, mla_kv_norm, mla_w_ukv, mla_q_head_norm, mla_k_head_norm,
              mla_out_norm, conv_w, conv_out_norm, w_out,
              ffn2_norm, ffn2_w_gate, ffn2_w_up, ffn2_w_down):
    pts = split_points(IN_SIZES)
    for l in range(DEPTH_2):
        x = x + 0.5 * swiglu(rms_norm_2(x, ffn1_norm[l]), ffn1_w_gate[l], ffn1_w_up[l], ffn1_w_down[l])
        h = rms_norm_2(x, mix_norm[l])
        u = h @ w_in[l]
        z, xbc, dt_raw, q_lat, kv_lat, k_pe, c_h, c_b, c_c = jnp.split(u, pts, axis=-1)
        y_ssd = ssd_mixer(z, xbc, dt_raw, ssd_conv_w[l], ssd_conv_b[l], ssd_dt_bias[l],
                          ssd_a_log[l], ssd_d[l], ssd_norm[l])
        y_mla = mla_mixer(q_lat, kv_lat, k_pe, positions, mla_q_norm[l], mla_w_uq[l], mla_kv_norm[l],
                          mla_w_ukv[l], mla_q_head_norm[l], mla_k_head_norm[l], mla_out_norm[l])
        y_conv = conv_mixer(c_h, c_b, c_c, conv_w[l], conv_out_norm[l])
        x = x + jnp.concatenate([y_ssd, y_mla, y_conv], axis=-1) @ w_out[l]
        x = x + 0.5 * swiglu(rms_norm_2(x, ffn2_norm[l]), ffn2_w_gate[l], ffn2_w_up[l], ffn2_w_down[l])
    return x


def setup_inputs(seed=0):
    out = dict(first_inputs(seed))
    for name, value in second_inputs(seed + 1).items():
        if name != "x":
            out[name + "_2"] = value
    return out


def reference(
    x, attn_norm, w_in, hg_lb_logits, hg_norm, fox_f_bias, fox_norm, w_out, ffn_norm, w_group,
    b_group, w_expert, b_expert, w_gate, w_up, w_down, final_norm, positions_2, ffn1_norm_2,
    ffn1_w_gate_2, ffn1_w_up_2, ffn1_w_down_2, mix_norm_2, w_in_2, ssd_conv_w_2, ssd_conv_b_2,
    ssd_dt_bias_2, ssd_a_log_2, ssd_d_2, ssd_norm_2, mla_q_norm_2, mla_w_uq_2, mla_kv_norm_2,
    mla_w_ukv_2, mla_q_head_norm_2, mla_k_head_norm_2, mla_out_norm_2, conv_w_2,
    conv_out_norm_2, w_out_2, ffn2_norm_2, ffn2_w_gate_2, ffn2_w_up_2, ffn2_w_down_2,
):
    x = first_block(
        x, attn_norm, w_in, hg_lb_logits, hg_norm, fox_f_bias, fox_norm, w_out, ffn_norm,
        w_group, b_group, w_expert, b_expert, w_gate, w_up, w_down, final_norm,
    )
    return second_block(
        x, positions_2, ffn1_norm_2, ffn1_w_gate_2, ffn1_w_up_2, ffn1_w_down_2, mix_norm_2,
        w_in_2, ssd_conv_w_2, ssd_conv_b_2, ssd_dt_bias_2, ssd_a_log_2, ssd_d_2, ssd_norm_2,
        mla_q_norm_2, mla_w_uq_2, mla_kv_norm_2, mla_w_ukv_2, mla_q_head_norm_2,
        mla_k_head_norm_2, mla_out_norm_2, conv_w_2, conv_out_norm_2, w_out_2, ffn2_norm_2,
        ffn2_w_gate_2, ffn2_w_up_2, ffn2_w_down_2,
    )


_drawn_inputs = setup_inputs


def setup_inputs(seed=0):
    import zlib

    import numpy as np

    out = dict(_drawn_inputs(seed))
    spreads = {}
    factors = {'hg_norm': 2.831,
     'b_expert': 3.204,
     'mla_q_norm_2': 2.732,
     'mla_k_head_norm_2': 2.678,
     'b_group': 3.161}
    for name, (base, spread) in spreads.items():
        noise = np.random.default_rng([zlib.crc32(name.encode()), seed]).standard_normal(out[name].shape)
        drawn = base * np.exp(spread * noise) if base else spread * noise
        out[name] = __import__('jax').numpy.asarray(drawn.astype(out[name].dtype))
    for name, factor in factors.items():
        out[name] = (out[name] * factor).astype(out[name].dtype)
    return out
```

```python
from contextlib import ExitStack

import numpy as np

import concourse.bass as bass
from concourse import mybir

F32 = mybir.dt.float32
F32R = mybir.dt.float32r
BF16 = mybir.dt.bfloat16
U32 = mybir.dt.uint32
I32 = mybir.dt.int32
ALU = mybir.AluOpType
ACT = mybir.ActivationFunctionType
AX = mybir.AxisListType

P = 128
S = 256
NT = S // P
D = 1024
KD = D // P
UNIT = 2048
RING = 3
EPS = 1e-6
BIG = 1e30

HH, HDK = 4, 128
FH, FDH = 8, 64
NG, NE = 4, 16
EF = 512
BLK = 256
MOE_BLOCKS = NE * EF // BLK
LEVELS = 7

LAYERS = 2
DFF = 2816
FFN_BLOCKS = DFF // BLK
SH, SP_, SG, SN = 16, 64, 2, 128
XT = 12
XC = 8
AH, AQK, AV, NOPE, ROPE = 8, 96, 64, 64, 32
QL, KVL = 256, 128
CT = 4

U_IN1 = 0
U_OUT1 = U_IN1 + 7 * 2
U_MOE = U_OUT1 + 4
U_LAYER = U_MOE + 3 * MOE_BLOCKS
L_FFN1 = 0
L_IN = L_FFN1 + 3 * FFN_BLOCKS
L_MLA = L_IN + 9 * 2
L_OUT = L_MLA + 1
L_FFN2 = L_OUT + 8
L_UNITS = L_FFN2 + 3 * FFN_BLOCKS
N_UNITS = U_LAYER + LAYERS * L_UNITS

PARAMS = [
    ("ident", P), ("causal", 2 * P), ("future", P),
    ("half_scale", 2), ("desc4", 4), ("row_sign", 1), ("row_back", 1), ("inv_freq", ROPE // 2),
    ("attn_gain", KD), ("ffn_gain", KD), ("lb_logits", 2 * HH), ("hg_gain", HDK), ("fox_gain", FDH),
    ("fox_bias", FH), ("router_bias", NG + NE), ("small_w", KD * (FH + NG + NE)),
]
LAYER_PARAMS = [
    ("ffn1_gain", KD), ("mix_gain", KD), ("ffn2_gain", KD), ("conv5_w", XT * 5), ("conv5_b", XT),
    ("dt_bias", 2 * SH), ("a_log", 2 * SH), ("d_skip", SH), ("ssd_gain", D), ("q_gain", 2), ("kv_gain", 1),
    ("qh_gain", AQK), ("kh_gain", AQK), ("mla_gain", AH * AV), ("conv3_w", CT * 3), ("conv_gain", 512),
    ("ukv_w", 512),
]


def offsets(table):
    at, out = 0, {}
    for name, width in table:
        out[name] = (at, width)
        at += width
    return out, at


P_AT, P_COLS = offsets(PARAMS)
LP_AT, LP_COLS = offsets(LAYER_PARAMS)


ROUND = 12582912.0
TURN = 2 * np.pi
TURN_HI = 6.28125
TURN_LO = TURN - TURN_HI
PI_BELOW = 3.1415925
SMALL = KD * (FH + NG + NE)
ARENA = 13400

COUNTS = {
    "x_ready": (3, 3), "norm_root": (3, 3), "normed": (2, 3), "flip": (12, 22), "xh_ready": (12, 22),
    "xl_ready": (12, 22), "sq": (2, 3), "sq_sum": (2, 3), "root": (2, 3),
}


def two_blocks(nc, stream, x_in, positions, prm_in, mask_in, final_in, lprm_in, out, stop=None):
    with ExitStack() as ctx:
        def sb(name, shape, dt=F32):
            return ctx.enter_context(nc.sbuf_tensor(name, shape, dt))

        sems = {}

        def ev(name):
            if name not in sems:
                sems[name] = ctx.enter_context(nc.semaphore(name))
            return sems[name]

        def at(name, k, l=None):
            before, each = COUNTS.get(name, (0, 1))
            return k if l is None else before + each * l + k

        raw = [sb(f"raw{i}", [P, UNIT]) for i in range(RING)]
        hi = [sb(f"hi{i}", [P, UNIT], F32R) for i in range(RING)]
        lo = [sb(f"lo{i}", [P, UNIT], F32R) for i in range(RING)]
        xh = sb("xh", [P, 2 * KD, S], F32R)
        xl = sb("xl", [P, 2 * KD, S], F32R)
        x = sb("x", [P, NT, D])
        mix = sb("mix", [P, NT * 2 * D])
        prm = sb("prm", [P, P_COLS])
        lprm = sb("lprm", [P, LP_COLS])
        small_hi = sb("small_hi", [P, 512], F32R)
        small_lo = sb("small_lo", [P, 512], F32R)
        stats = sb("stats", [P, 64])
        hth = sb("hth", [P, 2, S], F32R)
        htl = sb("htl", [P, 2, S], F32R)
        gates = sb("gates", [P, NT, NE, 2])
        route = sb("route", [P, 640])
        trig = sb("trig", [P, 2 * NT * ROPE // 2])
        pos = sb("pos", [P, NT], I32)
        arena = sb("arena", [P, ARENA])
        bank = [ctx.enter_context(nc.psum_tensor(f"bank{i}", [P, 512], F32)) for i in range(8)]

        def par(name):
            a, width = P_AT[name]
            return prm[:, a:a + width]

        def lpar(name):
            a, width = LP_AT[name]
            return lprm[:, a:a + width]

        def mix_part(a, width, row):
            return mix[:, 0:NT * row].rearrange("p (t d) -> p t d", d=row)[:, :, a:a + width]

        def area(a, width):
            assert a + width <= ARENA
            return arena[:, a:a + width]

        sil = mix[:, 0:NT * BLK].rearrange("p (t f) -> p t f", t=NT)
        hid = mix[:, NT * BLK:2 * NT * BLK].rearrange("p (t f) -> p t f", t=NT)
        ident = par("ident")
        eps_col, one_col = stats[:, 0:1], stats[:, 1:2]
        sumsq, root, rstd = stats[:, 8:10], stats[:, 10:12], stats[:, 12:14]

        hq, hk, hb = area(0, 1024), area(1024, 1024), area(2048, 1024)
        decay = [area(3072, 1024), area(4096, 1024)]
        score, cross = area(5120, 1024), area(6144, 512)
        hv, hg = area(6656, 1024), area(7680, 1024)
        fk, fv = area(8704, 1024), area(9728, 1024)
        level_mask, restart = area(10752, 1024), area(11776, 1024)
        fq = mix[:, 2048:4096]
        logit = [area(0, 1024), area(1024, 2048)]
        probT = area(3072, 3072)
        fcum, flog = area(6144, 256), area(6400, 256)

        final_gain = area(0, D)

        conv_in = area(0, XT * (S + 4)).rearrange("p (c t) -> p c t", t=S + 4)
        xs, cb_score = area(0, 2048), area(2048, 1024)
        zs = area(3120, 2048)
        misc = area(5168, 896).rearrange("p (t n) -> p t n", t=NT)
        prod = area(6064, CT * (S + 2)).rearrange("p (c t) -> p c t", t=S + 2)
        gate_b = area(7096, 1024)
        xbc = area(8120, XT * S)
        expo = [area(11192, 768), area(11960, 768)]
        c_in = area(11192, 1024)
        rows = area(12728, S)
        xd_f = area(8120, 2048)
        gains_q = lprm[:, LP_AT["q_gain"][0]:LP_AT["q_gain"][0] + 3]
        dt, dt_tmp, dt_a, row_cols = route[:, 0:64], route[:, 64:128], route[:, 128:192], route[:, 192:256]
        a_exp = route[:, 256:288]
        qk = area(0, 3072)
        qk_sq = area(3072, 3072)
        prob, prob_t = [area(0, 2048), area(2048, 2048)], [area(4096, 2048), area(6144, 2048)]
        va, q_t, k_t = area(8192, 1024), area(9216, 2048), area(11264, 2048)
        qk_sum, qk_root, qk_rstd = route[:, 288:320], route[:, 320:352], route[:, 352:384]
        peak, total = route[:, 384:400], route[:, 400:416]
        ob_rstd = route[:, 416:432]

        raw_in = [ev(f"raw_in{i}") for i in range(RING)]
        hi_done, lo_done, consumed = ev("hi_done"), ev("lo_done"), ev("consumed")

        class Chain:

            def __init__(self, eng, name):
                self.eng, self.sem, self.n = eng, ev(name), 0

            def __call__(self, ins):
                ins.then_inc(self.sem, 1)
                self.n += 1
                self.eng.wait_ge(self.sem, self.n)

        block = ctx.enter_context(nc.Block())

        @block.sync
        def _(sp):
            sp.dma_start(prm[:, :], prm_in).then_inc(ev("params_in"), 16)
            sp.dma_start(x[:, :, :], x_in.rearrange("(t p) d -> p t d", p=P)).then_inc(ev("x_in"), 16)
            sp.dma_start(pos[:, :], positions).then_inc(ev("pos_in"), 16)
            sp.dma_start(lprm[:, :], lprm_in[0]).then_inc(ev("lprm_in"), 16)
            sp.dma_start(level_mask, mask_in).then_inc(ev("mask_in"), 16)
            for n in range(RING):
                sp.dma_start(raw[n][:, :], stream[n]).then_inc(raw_in[n], 16)
            groups = N_UNITS // RING if stop is None else (stop + RING) // RING
            with sp.Fori(1, groups) as g:
                for s in range(RING):
                    sp.wait_ge(lo_done, (g - 1) * RING + s + 1)
                    sp.dma_start(raw[s][:, :],
                                 stream[bass.ds(g * RING + s, 1)].rearrange("o p n -> (o p) n")
                                 ).then_inc(raw_in[s], 16)
            sp.wait_ge(ev("result"), 1)
            sp.dma_start(out.rearrange("(t p) d -> p t d", p=P), x[:, :, :]).then_inc(ev("stored"), 16)
            sp.wait_ge(ev("stored"), 16)

        @block.scalar
        def _(act):
            chain = Chain(act, "act_chain")
            A = nc.scalar.activation

            def split_at(n, slot, group):
                act.wait_ge(raw_in[slot], (group + 1) * 16)
                if not isinstance(n, int) or n >= RING:
                    act.wait_ge(consumed, n - RING + 1)
                A(hi[slot][:, :], raw[slot][:, :], ACT.Copy).then_inc(hi_done, 1)

            def split(n):
                if n < N_UNITS and (stop is None or n < (stop + RING) // RING * RING):
                    split_at(n, n % RING, n // RING)

            def root_of(tag, ncols, width, l=None):
                act.wait_ge(ev("sq_sum"), at("sq_sum", tag, l))
                A(stats[:, 32:32 + ncols], stats[:, 16:16 + ncols], ACT.Sqrt, scale=1.0 / width,
                  bias=eps_col).then_inc(ev("root"), 1)

            def norm(k, gain, pairs, l=None):
                row_norm(k, l)
                to_operand(pairs, gain, KD, l)

            def row_norm(k, l=None):
                if k or l is not None:
                    act.wait_ge(ev("x_ready"), at("x_ready", k, l))
                for t in range(NT):
                    ins = A(mix[:, t * D:(t + 1) * D], x[:, t, :], ACT.Square, accum_out=sumsq[:, t:t + 1])
                chain(ins)
                A(root, sumsq, ACT.Sqrt, scale=1.0 / D, bias=eps_col).then_inc(ev("norm_root"), 1)

            def to_operand(pairs, gain, count, l=None):
                for j in range(count):
                    if j % 2 == 0:
                        act.wait_ge(ev("flip"), at("flip", pairs + j // 2 + 1, l))
                    src = bank[4 + (j // 2) % 4]
                    if gain is None:
                        if j % 2 == 0:
                            A(xh[:, j:j + 2, :], src[:, :], ACT.Copy).then_inc(ev("xh_ready"), 1)
                        continue
                    ins = A(xh[:, j, :], src[:, (j % 2) * S:(j % 2 + 1) * S], ACT.Copy, scale=gain[:, j:j + 1])
                    if j % 2 or j == count - 1:
                        ins.then_inc(ev("xh_ready"), 1)

            def ffn(base, g0, nb, blk0):
                def silu(b):
                    for t in range(NT):
                        ins = A(sil[:, t, :], bank[4 + t][:, 0:BLK], ACT.Silu)
                    ins.then_inc(ev("silu"), 1)

                def hidden(b):
                    act.wait_ge(ev("hid_flip"), b + blk0 + 1)
                    A(hth[:, :, :], bank[6][:, :], ACT.Copy).then_inc(ev("hth_ready"), 1)

                split_at(base + 3, 0, g0 + 1)
                act.wait_ge(consumed, base + 2)
                silu(0)
                split_at(base + 4, 1, g0 + 1)
                hidden(0)

                def body(b):
                    split_at(b * 3 + base + 2, 2, b + g0)
                    act.wait_ge(consumed, b * 3 + base + 1)
                    silu(b)
                    split_at(b * 3 + base + 3, 0, b + g0 + 1)
                    split_at(b * 3 + base + 4, 1, b + g0 + 1)
                    hidden(b)
                body(1)
                final = base + 3 * nb == N_UNITS
                with act.Fori(2, nb - final) as b:
                    body(b)
                if final:
                    split(N_UNITS - 1)
                    act.wait_ge(consumed, N_UNITS - 2)
                    silu(nb - 1)
                    hidden(nb - 1)

            act.wait_ge(ev("params_in"), 16)
            A(small_hi[:, 0:SMALL], par("small_w"), ACT.Copy).then_inc(ev("small_hi"), 1)
            for n in range(RING):
                split(n)
            act.wait_ge(ev("consts"), 1)
            act.wait_ge(ev("x_in"), 16)
            norm(0, par("attn_gain"), 0)
            act.wait_ge(ev("lb_diff"), 1)
            A(stats[:, 48:52], stats[:, 4:8], ACT.Sigmoid).then_inc(ev("lb"), 1)
            for c in range(7):
                split(2 * c + 3)
                split(2 * c + 4)
                act.wait_ge(consumed, 2 * c + 2)
                pair = [0, 2, 4, 6, 0, 2, 4][c]
                for i in range(2):
                    src = bank[pair + i]
                    part = slice(i * 512, (i + 1) * 512)
                    if c == 4:
                        for half in range(2):
                            dst = fq.rearrange("p (j h t) -> p j h t", h=2, t=S)[:, 2 * i:2 * i + 2, half, :]
                            ins = A(dst, src[:, :].rearrange("p (j t) -> p j t", t=S), ACT.Copy,
                                    scale=par("half_scale")[:, half:half + 1])
                        continue
                    dst, func = [(hq, ACT.Silu), (decay[0], ACT.Sigmoid), (hv, ACT.Copy), (hg, ACT.Silu),
                                 None, (fk, ACT.Copy), (fv, ACT.Copy)][c]
                    ins = A(dst[:, part], src[:, :], func)
                ins.then_inc(ev("u_out"), 1)
            act.wait_ge(ev("f_ready"), 1)
            A(decay[0], decay[1], ACT.Ln).then_inc(ev("log_f"), 1)
            for i in range(1, LEVELS + 2):
                act.wait_ge(ev("diff"), i)
                A(decay[i % 2], decay[i % 2], ACT.Exp).then_inc(ev("decay"), 1)
            act.wait_ge(ev("hg_o"), 1)
            for t in range(NT):
                ins = A(decay[0][:, t * 512:(t + 1) * 512], bank[4 + t][:, :], ACT.Square)
            ins.then_inc(ev("sq"), 1)
            root_of(1, NT * HH, HDK)
            act.wait_ge(ev("fox_x"), 1)
            chain(A(route[:, 16:32], route[:, 0:16], ACT.Abs))
            chain(A(route[:, 16:32], route[:, 16:32], ACT.Exp, scale=-1.0))
            A(route[:, 16:32], route[:, 16:32], ACT.Ln, bias=one_col).then_inc(ev("fox_ln"), 1)
            for t in range(NT):
                act.wait_ge(ev("fox_sub"), t + 1)
                A(logit[t], logit[t], ACT.Exp).then_inc(ev("fox_exp"), 1)
            for g in range(6):
                act.wait_ge(ev("fox_flip"), g + 1)
                A(probT[:, g * 512:(g + 1) * 512], bank[g][:, :], ACT.Copy).then_inc(ev("fox_pT"), 1)
            act.wait_ge(ev("fox_norm"), 1)
            A(logit[0].rearrange("p (t d) -> p t d", t=NT), mix_part(512, 512, D), ACT.Square).then_inc(ev("sq"), 1)
            root_of(2, NT * FH, FDH)
            to_operand(4, None, KD)
            for i in range(4):
                split(U_OUT1 + i + RING)
            norm(1, par("ffn_gain"), 8)
            act.dma_start(final_gain, final_in.to_broadcast([P, D])).then_inc(ev("final_in"), 16)
            act.wait_ge(ev("route_g"), 1)
            A(route[:, 48:56], route[:, 40:48], ACT.Exp).then_inc(ev("route_ge"), 1)
            act.wait_ge(ev("route_e"), 1)
            A(route[:, 120:122], route[:, 118:120], ACT.Exp).then_inc(ev("route_ee"), 1)
            ffn(U_MOE, U_MOE // RING, MOE_BLOCKS, 0)
            split(U_LAYER + 2)
            row_norm(2)

            def layer(l):
                u0 = U_LAYER + L_UNITS * l
                blk = MOE_BLOCKS + 2 * FFN_BLOCKS * l
                act.wait_ge(ev("lprm_in"), 16 * (l + 1))
                norm(0, lpar("ffn1_gain"), 0, l)
                ffn(u0, u0 // RING, FFN_BLOCKS, blk)
                split(u0 + L_IN + 2)
                A(small_hi[:, :], lpar("ukv_w"), ACT.Copy).then_inc(ev("ukv_hi"), 1)
                norm(1, lpar("mix_gain"), 4, l)
                for c in range(9):
                    split(u0 + L_IN + 2 * c + 3)
                    split(u0 + L_IN + 2 * c + 4)
                    if 1 <= c <= 3:
                        act.wait_ge(ev("conv5"), 3 * l + c)
                        for i in range(4 * c - 4, 4 * c):
                            ins = A(xbc[:, i * S:(i + 1) * S], xbc[:, i * S:(i + 1) * S], ACT.Silu,
                                    bias=lpar("conv5_b")[:, i:i + 1])
                        ins.then_inc(ev("xbc"), 1)
                    if c == 5:
                        continue
                    act.wait_ge(consumed, u0 + L_IN + 2 * c + 2)
                    for i in range(2):
                        src = bank[[0, 2, 4, 6, 0, 2, 4, 6, 0][c] + i]
                        if c < 3:
                            ins = A(conv_in[:, 4 * c + 2 * i:4 * c + 2 * i + 2, 2:S + 2],
                                    src[:, :].rearrange("p (c t) -> p c t", t=S), ACT.Copy)
                        elif c == 3:
                            ins = A(misc[:, i, :], src[:, 0:448], ACT.Copy)
                        elif c < 7:
                            ins = A((c_in if c == 4 else gate_b)[:, i * 512:(i + 1) * 512], src[:, :], ACT.Copy)
                        else:
                            ins = A(zs[:, i * D + (c - 7) * 512:i * D + (c - 6) * 512], src[:, :], ACT.Silu)
                    ins.then_inc(ev("u_part"), 1)
                act.wait_ge(ev("dt_x"), l + 1)
                chain(A(dt_tmp, dt, ACT.Abs))
                chain(A(dt_tmp, dt_tmp, ACT.Exp, scale=-1.0))
                A(a_exp, lpar("a_log"), ACT.Exp)
                A(dt_tmp, dt_tmp, ACT.Ln, bias=one_col).then_inc(ev("dt_ln"), 1)
                act.wait_ge(ev("xs_flip"), l + 1)
                for t in range(NT):
                    for i in range(2):
                        ins = A(xs[:, t * D + i * 512:t * D + (i + 1) * 512], bank[2 * t + i][:, :], ACT.Copy)
                ins.then_inc(ev("xs"), 1)
                act.wait_ge(ev("cb"), l + 1)
                for g in range(SG):
                    ins = A(cb_score[:, g * 512:(g + 1) * 512], bank[4 + g][:, :], ACT.Copy)
                ins.then_inc(ev("cb_out"), 1)
                act.wait_ge(ev("row_cols"), l + 1)
                for h in range(SH):
                    act.wait_ge(ev("expo"), SH * l + h + 1)
                    if h >= 2:
                        act.wait_ge(ev("y_head"), SH * l + h - 1)
                    e, b0, b1 = expo[h % 2], bank[2 * (h % 2)], bank[2 * (h % 2) + 1]
                    fwd = [row_cols[:, 32 * t + h:32 * t + h + 1] for t in range(NT)]
                    bwd = [row_cols[:, 32 * t + SH + h:32 * t + SH + h + 1] for t in range(NT)]
                    A(e[:, 0:256], b0[:, 0:256], ACT.Exp, bias=fwd[0])
                    A(e[:, 256:384], b0[:, 256:384], ACT.Exp, bias=bwd[0])
                    A(e[:, 384:640], b1[:, 0:256], ACT.Exp, bias=bwd[1])
                    A(e[:, 640:768], b1[:, 256:384], ACT.Exp, bias=fwd[1]).then_inc(ev("decays"), 1)
                act.wait_ge(ev("conv_y"), l + 1)
                A(area(6064, 1024), gate_b, ACT.Square).then_inc(ev("sq"), 1)
                root_of(1, 16, 64, l)
                act.wait_ge(ev("ssd_y"), l + 1)
                A(area(8120, 2048).rearrange("p (t d) -> p t d", t=NT), mix_part(0, D, 2 * D), ACT.Square).then_inc(ev("sq"), 1)
                root_of(2, 4, 512, l)
                for t in range(NT):
                    A(area(11192 + 256 * t, 256), misc[:, t, 32:288], ACT.Square, accum_out=stats[:, 56 + t:57 + t])
                    ins = A(area(11704 + 128 * t, 128), misc[:, t, 288:416], ACT.Square, accum_out=stats[:, 58 + t:59 + t])
                chain(ins)
                A(stats[:, 60:62], stats[:, 56:58], ACT.Sqrt, scale=1.0 / QL, bias=eps_col)
                A(stats[:, 62:64], stats[:, 58:60], ACT.Sqrt, scale=1.0 / KVL, bias=eps_col).then_inc(ev("lat_root"), 1)
                to_operand(8, gains_q, 3, l)
                act.wait_ge(consumed, u0 + L_MLA + 1)
                act.wait_ge(ev("kv_done"), l + 1)
                k4 = qk[:, 1536:3072].rearrange("p (t h d) -> p t h d", t=NT, d=AQK)
                for t in range(NT):
                    A(qk[:, t * 768:t * 768 + 512], bank[2 * t][:, :], ACT.Copy)
                    A(qk[:, t * 768 + 512:(t + 1) * 768], bank[2 * t + 1][:, 0:256], ACT.Copy)
                    for i in range(2):
                        kv = bank[4 + t + 2 * i][:, :].rearrange("p (h d) -> p h d", d=NOPE + AV)
                        A(k4[:, t, 4 * i:4 * i + 4, 0:NOPE], kv[:, :, 0:NOPE], ACT.Copy)
                        A(va[:, t * 512 + i * 256:t * 512 + (i + 1) * 256].rearrange("p (h d) -> p h d", d=AV),
                          kv[:, :, NOPE:], ACT.Copy)
                    ins = A(k4[:, t, :, NOPE:], misc[:, t, 416:448].unsqueeze(1).to_broadcast([P, AH, ROPE]), ACT.Copy)
                chain(ins)
                split(u0 + L_IN + 21)
                A(qk_sq, qk, ACT.Square).then_inc(ev("qk_sq"), 1)
                act.wait_ge(ev("qk_sum"), l + 1)
                A(qk_root, qk_sum, ACT.Sqrt, scale=1.0 / AQK, bias=eps_col).then_inc(ev("qk_root"), 1)
                for g in range(8):
                    act.wait_ge(ev("qk_flip"), 8 * l + g + 1)
                    dst = (q_t if g < 4 else k_t)[0:AQK, (g % 4) * 512:(g % 4 + 1) * 512]
                    ins = A(dst, bank[g][0:AQK, :], ACT.Copy)
                    ins.then_inc(ev("qk_t"), 1)
                for t in range(NT):
                    act.wait_ge(ev("peak"), 2 * l + t + 1)
                    for h in range(AH):
                        i = AH * t + h
                        ins = A(prob[t][:, h * S:(h + 1) * S], bank[4 * t + h // 2][:, (h % 2) * S:(h % 2 + 1) * S], ACT.Exp,
                                scale=AQK ** -0.5, bias=peak[:, i:i + 1], accum_out=total[:, i:i + 1])
                    ins.then_inc(ev("prob"), 1)
                for g in range(8):
                    act.wait_ge(ev("prob_flip"), 8 * l + g + 1)
                    A(prob_t[g // 4][:, (g % 4) * 512:(g % 4 + 1) * 512], bank[g][:, :], ACT.Copy).then_inc(ev("prob_t"), 1)
                act.wait_ge(ev("mla_y"), l + 1)
                A(area(0, 1024).rearrange("p (t d) -> p t d", t=NT), mix_part(D, 512, 2 * D), ACT.Square).then_inc(ev("sq"), 1)
                root_of(3, 16, AV, l)
                to_operand(10, None, 2 * KD, l)
                for i in range(8):
                    split(u0 + L_OUT + i + RING)
                norm(2, lpar("ffn2_gain"), 18, l)
                if l + 1 < LAYERS:
                    act.wait_ge(ev("xl_ready"), at("xl_ready", 22, l))
                    act.dma_start(lprm[:, :], lprm_in[l + 1]).then_inc(ev("lprm_in"), 16)
                ffn(u0 + L_FFN2, (u0 + L_FFN2) // RING, FFN_BLOCKS, blk + FFN_BLOCKS)
                split(u0 + L_UNITS + 2)

            if stop is None or stop > U_LAYER + 5:
                act.wait_ge(ev("trig_arg"), 1)
                A(trig[:, :], trig[:, :], ACT.Sin).then_inc(ev("trig"), 1)
                for l in range(LAYERS):
                    layer(l)

        @block.vector
        def _(dve):
            V = nc.vector
            chain = Chain(dve, "dve_chain")

            def tt(o, a, b, op):
                return V.tensor_tensor(o, a, b, op)

            def split_at(n, slot):
                dve.wait_ge(hi_done, n + 1)
                tt(lo[slot][:, :], raw[slot][:, :], hi[slot][:, :].bitcast(F32), ALU.subtract).then_inc(lo_done, 1)

            def split(n):
                if n < N_UNITS and (stop is None or n < (stop + RING) // RING * RING):
                    split_at(n, n % RING)

            def norm(k, gain, pairs, l=None):
                scale_rows(k, l)
                to_operand(pairs, gain, KD, l)

            def scale_rows(k, l=None):
                dve.wait_ge(ev("norm_root"), at("norm_root", k + 1, l))
                chain(V.reciprocal(rstd, root))
                for t in range(NT):
                    ins = V.tensor_scalar(mix[:, t * D:(t + 1) * D], x[:, t, :], rstd[:, t:t + 1], None, ALU.mult)
                ins.then_inc(ev("normed"), 1)

            def to_operand(pairs, gain, count, l=None):
                for j in range(count):
                    if j % 2 == 0:
                        dve.wait_ge(ev("xh_ready"), at("xh_ready", pairs + j // 2 + 1, l))
                    src = bank[4 + (j // 2) % 4]
                    if gain is None:
                        if j % 2 == 0:
                            tt(xl[:, j:j + 2, :], src[:, :].rearrange("p (j t) -> p j t", t=S),
                               xh[:, j:j + 2, :].bitcast(F32), ALU.subtract).then_inc(ev("xl_ready"), 1)
                        continue
                    ins = V.scalar_tensor_tensor(xl[:, j, :], src[:, (j % 2) * S:(j % 2 + 1) * S], gain[:, j:j + 1],
                                                 xh[:, j, :].bitcast(F32), ALU.mult, ALU.subtract)
                    if j % 2 or j == count - 1:
                        ins.then_inc(ev("xl_ready"), 1)

            def rms(values, squares, heads, width, tag, l=None):
                dve.wait_ge(ev("sq"), at("sq", tag, l))
                V.tensor_reduce(stats[:, 16:16 + heads], squares, AX.X, ALU.add).then_inc(ev("sq_sum"), 1)
                dve.wait_ge(ev("root"), at("root", tag, l))
                chain(V.reciprocal(values, stats[:, 32:32 + heads]))

            def ffn(base, nb, blk0, gated):
                def hidden(b):
                    dve.wait_ge(ev("silu"), b + blk0 + 1)
                    for t in range(NT):
                        up = bank[4 + t][:, BLK:2 * BLK]
                        if gated:
                            gate = gates[:, t, :, :].rearrange("p e b -> p (e b)")[:, bass.ds(b, 1)]
                            ins = V.scalar_tensor_tensor(hid[:, t, :], sil[:, t, :], gate, up, ALU.mult, ALU.mult)
                        else:
                            ins = tt(hid[:, t, :], sil[:, t, :], up, ALU.mult)
                    ins.then_inc(ev("hid_ready"), 1)

                def rest(b):
                    dve.wait_ge(ev("hth_ready"), b + blk0 + 1)
                    tt(htl[:, :, :], bank[6][:, :].rearrange("p (f t) -> p f t", t=S),
                       hth[:, :, :].bitcast(F32), ALU.subtract).then_inc(ev("htl_ready"), 1)

                split_at(base + 3, 0)
                hidden(0)
                split_at(base + 4, 1)
                rest(0)

                def body(b):
                    split_at(b * 3 + base + 2, 2)
                    hidden(b)
                    split_at(b * 3 + base + 3, 0)
                    split_at(b * 3 + base + 4, 1)
                    rest(b)
                body(1)
                final = base + 3 * nb == N_UNITS
                with dve.Fori(2, nb - final) as b:
                    body(b)
                if final:
                    split(N_UNITS - 1)
                    hidden(nb - 1)
                    rest(nb - 1)

            def residual(n, scale):
                dve.wait_ge(consumed, n + 1)
                for t in range(NT):
                    for c in range(2):
                        part = x[:, t, c * 512:(c + 1) * 512]
                        ins = V.scalar_tensor_tensor(part, bank[2 * t + c][:, :], scale, part, ALU.mult, ALU.add)
                ins.then_inc(ev("x_ready"), 1)

            V.memset(eps_col, EPS)
            V.memset(one_col, 1.0)
            V.memset(restart, 1.0)
            chain(V.memset(score, 0.0))
            chain(V.memset(restart.rearrange("p (n t) -> p n t", t=P)[:, :, 0:1], 0.0))
            V.memset(stats[:, 2:3], 0.0).then_inc(ev("consts"), 1)
            dve.wait_ge(ev("params_in"), 16)
            dve.wait_ge(ev("small_hi"), 1)
            tt(small_lo[:, 0:SMALL], par("small_w"), small_hi[:, 0:SMALL].bitcast(F32), ALU.subtract).then_inc(ev("small_lo"), 1)
            for n in range(RING):
                split(n)
            lbl = par("lb_logits")
            norm(0, par("attn_gain"), 0)
            tt(stats[:, 4:8], lbl[:, 0:HH], lbl[:, HH:2 * HH], ALU.subtract).then_inc(ev("lb_diff"), 1)
            for c in range(7):
                split(2 * c + 3)
                split(2 * c + 4)
            dve.wait_ge(ev("lb"), 1)
            chain(V.tensor_scalar(stats[:, 52:56], stats[:, 48:52], -1.0, 1.0, ALU.mult, ALU.add))
            dve.wait_ge(ev("u_out"), 2)
            for h in range(HH):
                part = slice(h * S, (h + 1) * S)
                ins = V.tensor_scalar(decay[1][:, part], decay[0][:, part], stats[:, 52 + h:53 + h],
                                      stats[:, 48 + h:49 + h], ALU.mult, ALU.add)
            ins.then_inc(ev("f_ready"), 1)
            dve.wait_ge(ev("f_ready"), 1)
            chain(V.tensor_scalar(hk, decay[1], -1.0, 1.0, ALU.mult, ALU.add))
            dve.wait_ge(ev("log_f"), 1)
            chain(V.tensor_tensor_scan(hb, restart, decay[0], 0.0, ALU.mult, ALU.add))

            def halves(a, i):
                v = a.rearrange("p (n s t) -> p n s t", s=2, t=1 << (i - 1))
                return v[:, :, 0, :], v[:, :, 1, :]

            def diff(i):
                if i > 2:
                    dve.wait_ge(ev("level"), i - 1)
                w = 1 << (i - 1)
                n = 1024 // (2 * w)
                bl, br = halves(hb, i)
                dl, dr = halves(decay[i % 2], i)
                last = bl[:, :, w - 1:w].to_broadcast([P, n, w])
                tt(dl, last, bl, ALU.subtract)
                if i <= LEVELS:
                    ins = tt(dr, br, last, ALU.subtract)
                else:
                    ins = V.tensor_copy(dr, br)
                ins.then_inc(ev("diff"), 1)

            def weigh(i):
                dve.wait_ge(ev("decay"), i)
                dl, dr = halves(decay[i % 2], i)
                tt(dl, dl, halves(hk, i)[0], ALU.mult)
                tt(dr, dr, halves(hq, i)[1], ALU.mult).then_inc(ev("weighed"), 1)

            def keep(i):
                dve.wait_ge(ev("level"), i + 1)
                for g in range(2 if i <= LEVELS else 1):
                    src = bank[2 * (i % 2) + g][:, :]
                    if i > LEVELS:
                        ins = V.tensor_copy(cross, src)
                        continue
                    mask = level_mask[:, i * P:(i + 1) * P].bitcast(U32).unsqueeze(1).to_broadcast([P, 4, P])
                    ins = V.copy_predicated(score[:, g * 512:(g + 1) * 512].rearrange("p (n t) -> p n t", t=P),
                                            mask, src.rearrange("p (n t) -> p n t", t=P))
                ins.then_inc(ev("kept"), 1)
                dve.wait_ge(ev("kept"), i + 1)

            dve.wait_ge(ev("mask_in"), 16)
            diff(1)
            for i in range(1, LEVELS + 2):
                if i <= LEVELS:
                    diff(i + 1)
                weigh(i)
                keep(i - 1)
            keep(LEVELS + 1)
            rms(stats[:, 56:64], decay[0].rearrange("p (n d) -> p n d", d=HDK), NT * HH, HDK, 1)
            for t in range(NT):
                o3 = mix[:, t * D:t * D + 512].rearrange("p (n d) -> p n d", d=HDK)
                chain(tt(o3, bank[4 + t][:, :].rearrange("p (n d) -> p n d", d=HDK),
                         stats[:, 56 + 4 * t:60 + 4 * t].unsqueeze(2).to_broadcast([P, HH, HDK]), ALU.mult))
                chain(tt(o3, o3, par("hg_gain").unsqueeze(1).to_broadcast([P, HH, HDK]), ALU.mult))
                chain(tt(mix[:, t * D:t * D + 512], mix[:, t * D:t * D + 512], hg[:, t * 512:(t + 1) * 512], ALU.mult))

            dve.wait_ge(ev("fox_f"), 1)
            r3 = lambda a, n: route[:, a:a + NT * n].rearrange("p (t n) -> p t n", n=n)
            chain(tt(r3(0, FH), bank[6][:, 0:16].rearrange("p (t n) -> p t n", n=FH),
                     par("fox_bias").unsqueeze(1).to_broadcast([P, NT, FH]), ALU.add))
            V.tensor_scalar(route[:, 32:48], route[:, 0:16], 0.0, None, ALU.min).then_inc(ev("fox_x"), 1)
            dve.wait_ge(ev("fox_ln"), 1)
            tt(route[:, 32:48], route[:, 16:32], route[:, 32:48], ALU.subtract).then_inc(ev("fox_log"), 1)
            dve.wait_ge(ev("fox_log_flip"), 1)
            chain(V.memset(fcum, 0.0))
            chain(V.tensor_copy(flog[0:FH, :], bank[7][0:FH, 0:S]))
            V.tensor_tensor_scan(fcum[0:FH, :], one_col[0:FH, :].to_broadcast([FH, S]), flog[0:FH, :], 0.0, ALU.mult, ALU.add).then_inc(ev("fox_cum"), 1)
            dve.wait_ge(ev("fox_logits"), 1)
            causal = par("causal")
            for g in range(2):
                ins = tt(logit[0][:, g * 512:(g + 1) * 512].rearrange("p (h s) -> p h s", s=P),
                         bank[g][:, :].rearrange("p (h s) -> p h s", s=P), causal[:, P:S].unsqueeze(1).to_broadcast([P, 4, P]), ALU.add)
            for g in range(4):
                ins = tt(logit[1][:, g * 512:(g + 1) * 512].rearrange("p (h s) -> p h s", s=S),
                         bank[2 + g][:, :].rearrange("p (h s) -> p h s", s=S),
                         causal.unsqueeze(1).to_broadcast([P, 2, S]), ALU.add)
            chain(ins)
            for t in range(NT):
                w = P * (t + 1)
                z = logit[t].rearrange("p (h s) -> p h s", s=w)
                m = route[:, 64 + 8 * t:72 + 8 * t]
                chain(V.tensor_reduce(m, z, AX.X, ALU.max))
                tt(z, z, m.unsqueeze(2).to_broadcast([P, FH, w]), ALU.subtract).then_inc(ev("fox_sub"), 1)
            for t in range(NT):
                w = P * (t + 1)
                dve.wait_ge(ev("fox_exp"), t + 1)
                z = logit[t].rearrange("p (h s) -> p h s", s=w)
                chain(V.tensor_reduce(route[:, 80 + 8 * t:88 + 8 * t], z, AX.X, ALU.add))
            chain(V.reciprocal(route[:, 96:112], route[:, 80:96]))
            dve.wait_ge(ev("fox_o"), 1)
            for t in range(NT):
                ins = tt(mix[:, t * D + 512:(t + 1) * D].rearrange("p (h d) -> p h d", d=FDH),
                         bank[6 + t][:, :].rearrange("p (h d) -> p h d", d=FDH),
                         route[:, 96 + 8 * t:104 + 8 * t].unsqueeze(2).to_broadcast([P, FH, FDH]), ALU.mult)
            ins.then_inc(ev("fox_norm"), 1)
            dve.wait_ge(ev("fox_norm"), 1)
            rms(route[:, 112:128], logit[0].rearrange("p (n d) -> p n d", d=FDH), NT * FH, FDH, 2)
            for t in range(NT):
                o3 = mix[:, t * D + 512:(t + 1) * D].rearrange("p (h d) -> p h d", d=FDH)
                chain(tt(o3, o3, route[:, 112 + 8 * t:120 + 8 * t].unsqueeze(2).to_broadcast([P, FH, FDH]), ALU.mult))
                ins = tt(o3, o3, par("fox_gain").unsqueeze(1).to_broadcast([P, FH, FDH]), ALU.mult)
            ins.then_inc(ev("mixed"), 1)
            to_operand(4, None, KD)
            for i in range(4):
                split(U_OUT1 + i + RING)
            residual(U_OUT1 + 3, 1.0)
            norm(1, par("ffn_gain"), 8)

            dve.wait_ge(ev("routed"), 1)
            lg = r3(0, NG + NE)
            chain(tt(lg, bank[6][:, 0:2 * (NG + NE)].rearrange("p (t n) -> p t n", n=NG + NE),
                     par("router_bias").unsqueeze(1).to_broadcast([P, NT, NG + NE]), ALU.add))
            lgg = lg[:, :, 0:NG]
            desc = par("desc4").unsqueeze(1).to_broadcast([P, NT, 4])

            def best(values, peak, onehot, tmp):
                chain(V.tensor_reduce(peak, values, AX.X, ALU.max))
                chain(tt(tmp, values, peak.unsqueeze(2).to_broadcast([P, NT, 4]), ALU.is_equal))
                chain(tt(tmp, tmp, desc, ALU.mult))
                chain(V.tensor_reduce(route[:, 136:138], tmp, AX.X, ALU.max))
                chain(tt(onehot, tmp, route[:, 136:138].unsqueeze(2).to_broadcast([P, NT, 4]), ALU.is_equal))

            r4 = lambda a: route[:, a:a + 8].rearrange("p (t n) -> p t n", n=4)
            best(lgg, route[:, 56:58], r4(60), r4(68))
            tt(r4(40), lgg, route[:, 56:58].unsqueeze(2).to_broadcast([P, NT, 4]), ALU.subtract).then_inc(ev("route_g"), 1)
            picked = route[:, 144:176].rearrange("p (t e g) -> p t e g", t=NT, e=4)
            for t in range(NT):
                ins = tt(picked[:, t, :, :], lg[:, t, NG:NG + NE].rearrange("p (g e) -> p e g", e=4),
                         r4(60)[:, t, :].unsqueeze(1).to_broadcast([P, 4, 4]), ALU.mult)
            chain(ins)
            chain(V.tensor_reduce(route[:, 76:84], route[:, 144:176].rearrange("p (n g) -> p n g", g=4), AX.X, ALU.add))
            best(r4(76), route[:, 84:86], r4(88), r4(68))
            chain(V.scalar_tensor_tensor(route[:, 96:104], route[:, 88:96], -BIG, route[:, 76:84], ALU.mult, ALU.add))
            best(r4(96), route[:, 86:88], r4(104), r4(68))
            tt(route[:, 118:120], route[:, 86:88], route[:, 84:86], ALU.subtract).then_inc(ev("route_e"), 1)
            dve.wait_ge(ev("route_ge"), 1)
            chain(V.tensor_reduce(route[:, 112:114], r4(48), AX.X, ALU.add))
            dve.wait_ge(ev("route_ee"), 1)
            chain(V.tensor_scalar(route[:, 122:124], route[:, 120:122], 1.0, None, ALU.add))
            chain(tt(route[:, 122:124], route[:, 122:124], route[:, 112:114], ALU.mult))
            chain(V.reciprocal(route[:, 124:126], route[:, 122:124]))
            chain(tt(route[:, 126:128], route[:, 124:126], route[:, 120:122], ALU.mult))
            chain(tt(r4(88), r4(88), route[:, 124:126].unsqueeze(2).to_broadcast([P, NT, 4]), ALU.mult))
            chain(tt(r4(104), r4(104), route[:, 126:128].unsqueeze(2).to_broadcast([P, NT, 4]), ALU.mult))
            chain(tt(r4(88), r4(88), r4(104), ALU.add))
            for t in range(NT):
                for g in range(NG):
                    for e in range(2):
                        ins = tt(gates[:, t, 4 * g:4 * g + 4, e], r4(88)[:, t, :],
                                 r4(60)[:, t, g:g + 1].to_broadcast([P, 4]), ALU.mult)
            chain(ins)
            ffn(U_MOE, MOE_BLOCKS, 0, True)
            split(U_LAYER + 2)
            residual(U_LAYER - 1, 1.0)
            dve.wait_ge(ev("final_in"), 16)
            dve.wait_ge(ev("norm_root"), 3)
            chain(V.reciprocal(rstd, root))
            for t in range(NT):
                ins = V.scalar_tensor_tensor(x[:, t, :], x[:, t, :], rstd[:, t:t + 1], final_gain, ALU.mult, ALU.mult)
            if stop is not None:
                ins.then_inc(ev("result"), 1)
                return
            ins.then_inc(ev("x_ready"), 1)

            dve.wait_ge(ev("pos_in"), 16)
            chain(V.tensor_copy(route[:, 0:NT], pos[:, :]))
            half = ROPE // 2
            ang, turns = route[:, 16:16 + NT * half], route[:, 64:64 + NT * half]
            for t in range(NT):
                ins = V.tensor_scalar(ang[:, t * half:(t + 1) * half], par("inv_freq"), route[:, t:t + 1], None, ALU.mult)
            chain(ins)
            for i, (quarter, shift) in enumerate([(0.25, np.pi / 2), (0.0, 0.0)]):
                dst = trig[:, i * NT * half:(i + 1) * NT * half]
                chain(V.tensor_scalar(turns, ang, 1 / TURN, quarter, ALU.mult, ALU.add))
                chain(V.tensor_scalar(turns, turns, ROUND, ROUND, ALU.add, ALU.subtract))
                chain(V.scalar_tensor_tensor(dst, turns, -TURN_HI, ang, ALU.mult, ALU.add))
                chain(V.scalar_tensor_tensor(dst, turns, -TURN_LO, dst, ALU.mult, ALU.add))
                chain(V.tensor_scalar(dst, dst, float(shift), PI_BELOW, ALU.add, ALU.min))
                ins = V.tensor_scalar(dst, dst, -PI_BELOW, None, ALU.max)
                if i == 0:
                    chain(ins)
            ins.then_inc(ev("trig_arg"), 1)

            def layer(l):
                u0 = U_LAYER + L_UNITS * l
                blk = MOE_BLOCKS + 2 * FFN_BLOCKS * l
                dve.wait_ge(ev("lprm_in"), 16 * (l + 1))
                norm(0, lpar("ffn1_gain"), 0, l)
                ffn(u0, FFN_BLOCKS, blk, False)
                split(u0 + L_IN + 2)
                residual(u0 + L_IN - 1, 0.5)
                dve.wait_ge(ev("ukv_hi"), l + 1)
                tt(small_lo[:, :], lpar("ukv_w"), small_hi[:, :].bitcast(F32), ALU.subtract).then_inc(ev("ukv_lo"), 1)
                norm(1, lpar("mix_gain"), 4, l)
                V.memset(conv_in[:, :, 0:2], 0.0)
                V.memset(conv_in[:, :, S + 2:S + 4], 0.0)
                V.memset(prod[:, :, 0:1], 0.0)
                chain(V.memset(prod[:, :, S + 1:S + 2], 0.0))

                def taps(src, dst, w, tiles, count, signal):
                    for k in range(count):
                        for i in tiles:
                            o = dst[:, i * S:(i + 1) * S]
                            wk = w[:, i * count + k:i * count + k + 1]
                            if k == 0:
                                ins = V.tensor_scalar(o, src[:, i, 0:S], wk, None, ALU.mult)
                            else:
                                ins = V.scalar_tensor_tensor(o, src[:, i, k:k + S], wk, o, ALU.mult, ALU.add)
                        if k == count - 1:
                            ins.then_inc(signal, 1)
                        else:
                            chain(ins)

                for c in range(9):
                    split(u0 + L_IN + 2 * c + 3)
                    split(u0 + L_IN + 2 * c + 4)
                    if 1 <= c <= 3:
                        dve.wait_ge(ev("u_part"), 8 * l + c)
                        taps(conv_in, xbc, lpar("conv5_w"), range(4 * c - 4, 4 * c), 5, ev("conv5"))
                    if c == 5:
                        dve.wait_ge(ev("u_part"), 8 * l + 5)
                        dve.wait_ge(consumed, u0 + L_IN + 2 * c + 2)
                        for i in range(2):
                            ins = tt(prod[:, 2 * i:2 * i + 2, 1:S + 1], bank[2 + i][:, :].rearrange("p (c t) -> p c t", t=S),
                                     c_in[:, i * 512:(i + 1) * 512].rearrange("p (c t) -> p c t", t=S), ALU.mult)
                        ins.then_inc(ev("c_prod"), 1)
                        dve.wait_ge(ev("c_prod"), l + 1)
                        taps(prod, c_in, lpar("conv3_w"), range(CT), 3, ev("conv3"))
                m3 = lambda a: a.rearrange("p (t n) -> p t n", t=NT)
                chain(tt(m3(dt), misc[:, :, 0:32], lpar("dt_bias").unsqueeze(1).to_broadcast([P, NT, 32]), ALU.add))
                V.tensor_scalar(dt_a, dt, 0.0, None, ALU.max).then_inc(ev("dt_x"), 1)
                dve.wait_ge(ev("dt_ln"), l + 1)
                chain(tt(dt, dt_a, dt_tmp, ALU.add))
                V.scalar_tensor_tensor(m3(dt_a), m3(dt), -1.0, a_exp.unsqueeze(1).to_broadcast([P, NT, 32]),
                                       ALU.mult, ALU.mult).then_inc(ev("dt_a"), 1)
                dve.wait_ge(ev("dt_flip"), l + 1)
                rate, cum = mix[0:32, 0:S], mix[0:32, S:2 * S]
                V.memset(rows, 0.0)
                chain(V.tensor_copy(rate, bank[7][0:32, 0:S]))
                chain(V.tensor_tensor_scan(cum, one_col[0:32, :].to_broadcast([32, S]), rate, 0.0, ALU.mult, ALU.add))
                chain(V.tensor_scalar(cum, cum, par("row_sign")[0:32, :], None, ALU.mult))
                V.scalar_tensor_tensor(rows[0:32, :], rate, par("row_back")[0:32, :], cum, ALU.mult, ALU.add).then_inc(ev("rows"), 1)
                dve.wait_ge(ev("rows_flip"), l + 1)
                V.tensor_scalar(m3(row_cols), bank[7][:, 0:S].rearrange("p (t n) -> p t n", t=NT)[:, :, 0:32],
                                -1.0, None, ALU.mult).then_inc(ev("row_cols"), 1)
                dve.wait_ge(ev("c_flip"), l + 1)
                for t in range(NT):
                    part = gate_b[:, t * 512:(t + 1) * 512]
                    ins = tt(part, part, bank[6 if t == 0 else 3][:, :], ALU.mult)
                ins.then_inc(ev("conv_y"), 1)
                dve.wait_ge(ev("xs"), l + 1)

                def heads(a):
                    return a.rearrange("p (h d) -> p h d", d=SP_)

                for t in range(NT):
                    src = heads(xs[:, t * D:(t + 1) * D])
                    f, b = dt[:, 32 * t:32 * t + SH], dt[:, 32 * t + SH:32 * t + 32]
                    tt(heads(xd_f[:, t * D:(t + 1) * D]), src, f.unsqueeze(2).to_broadcast([P, SH, SP_]), ALU.mult)
                    ins = tt(heads(mix[:, t * 2 * D + D:(t + 1) * 2 * D]), src, b.unsqueeze(2).to_broadcast([P, SH, SP_]), ALU.mult)
                ins.then_inc(ev("xd"), 1)
                dve.wait_ge(ev("xd"), l + 1)
                for t in range(NT):
                    src = heads(xs[:, t * D:(t + 1) * D])
                    ins = tt(src, src, lpar("d_skip").unsqueeze(2).to_broadcast([P, SH, SP_]), ALU.mult)
                chain(ins)
                dve.wait_ge(ev("cb_out"), l + 1)
                for h in range(SH):
                    dve.wait_ge(ev("decays"), SH * l + h + 1)
                    e, g = expo[h % 2], h // 8
                    for c, s, l0, w in [(0, 0, 0, 256), (256, 0, 0, 128), (384, 1, 0, 256), (640, 1, 128, 128)]:
                        cc = g * 512 + s * 256 + l0
                        ins = tt(e[:, c:c + w], e[:, c:c + w], cb_score[:, cc:cc + w], ALU.mult)
                    ins.then_inc(ev("scores"), 1)
                def group_rms(values, squares, heads_, width, tag):
                    rms(values, squares, heads_, width, tag, l)
                group_rms(ob_rstd, area(6064, 1024).rearrange("p (n d) -> p n d", d=64), 16, 64, 1)
                g3 = gate_b.rearrange("p (n d) -> p n d", d=64)
                chain(tt(g3, g3, ob_rstd.unsqueeze(2).to_broadcast([P, 16, 64]), ALU.mult))
                dve.wait_ge(ev("y_head"), SH * (l + 1))
                for t in range(NT):
                    tt(mix[:, t * 2 * D + 1536:(t + 1) * 2 * D], gate_b[:, t * 512:(t + 1) * 512], lpar("conv_gain"), ALU.mult)
                for t in range(NT):
                    for i in range(2):
                        o = mix[:, t * 2 * D + i * 512:t * 2 * D + (i + 1) * 512]
                        ins = tt(o, bank[4 + 2 * t + i][:, :], xs[:, t * D + i * 512:t * D + (i + 1) * 512], ALU.add)
                chain(ins)
                y3 = mix_part(0, D, 2 * D)
                tt(y3, y3, zs.rearrange("p (t d) -> p t d", t=NT), ALU.mult).then_inc(ev("ssd_y"), 1)
                dve.wait_ge(ev("ssd_y"), l + 1)
                group_rms(ob_rstd[:, 0:4], area(8120, 2048).rearrange("p (n d) -> p n d", d=512), 4, 512, 2)
                for t in range(NT):
                    for i in range(2):
                        o = mix[:, t * 2 * D + i * 512:t * 2 * D + (i + 1) * 512]
                        ins = V.scalar_tensor_tensor(o, o, ob_rstd[:, 2 * t + i:2 * t + i + 1],
                                                     lpar("ssd_gain")[:, i * 512:(i + 1) * 512], ALU.mult, ALU.mult)
                chain(ins)
                dve.wait_ge(ev("lat_root"), l + 1)
                chain(V.reciprocal(stats[:, 56:60], stats[:, 60:64]))
                for t in range(NT):
                    V.tensor_scalar(misc[:, t, 32:288], misc[:, t, 32:288], stats[:, 56 + t:57 + t], None, ALU.mult)
                    ins = V.tensor_scalar(misc[:, t, 288:416], misc[:, t, 288:416], stats[:, 58 + t:59 + t], None, ALU.mult)
                ins.then_inc(ev("lat"), 1)
                to_operand(8, gains_q, 3, l)
                split(u0 + L_IN + 21)
                dve.wait_ge(ev("qk_sq"), l + 1)
                V.tensor_reduce(qk_sum, qk_sq.rearrange("p (n d) -> p n d", d=AQK), AX.X, ALU.add).then_inc(ev("qk_sum"), 1)
                dve.wait_ge(ev("qk_root"), l + 1)
                chain(V.reciprocal(qk_rstd, qk_root))
                n3 = qk.rearrange("p (n d) -> p n d", d=AQK)
                chain(tt(n3, n3, qk_rstd.unsqueeze(2).to_broadcast([P, 4 * AH, AQK]), ALU.mult))
                for i, name in enumerate(["qh_gain", "kh_gain"]):
                    part = n3[:, 16 * i:16 * (i + 1), :]
                    ins = tt(part, part, lpar(name).unsqueeze(1).to_broadcast([P, 16, AQK]), ALU.mult)
                chain(ins)
                half = ROPE // 2
                dve.wait_ge(ev("trig"), 1)
                q5 = qk.rearrange("p (i t h d) -> p i t h d", i=2, t=NT, d=AQK)
                for t in range(NT):
                    lo_, hi_ = q5[:, :, t, :, NOPE:NOPE + half], q5[:, :, t, :, NOPE + half:AQK]
                    tmp = [area(3072 + 256 * i, 256).rearrange("p (i h d) -> p i h d", i=2, d=half) for i in range(4)]

                    def turned(i):
                        a = trig[:, (i * NT + t) * half:(i * NT + t + 1) * half]
                        return a.unsqueeze(1).unsqueeze(1).to_broadcast([P, 2, AH, half])
                    tt(tmp[0], lo_, turned(0), ALU.mult)
                    tt(tmp[1], hi_, turned(1), ALU.mult)
                    tt(tmp[2], lo_, turned(1), ALU.mult)
                    chain(tt(tmp[3], hi_, turned(0), ALU.mult))
                    tt(lo_, tmp[0], tmp[1], ALU.subtract)
                    ins = tt(hi_, tmp[2], tmp[3], ALU.add)
                    if t == 0:
                        chain(ins)
                ins.then_inc(ev("qk"), 1)
                for t in range(NT):
                    dve.wait_ge(ev("logits"), 2 * l + t + 1)
                    for g in range(4):
                        ins = V.tensor_reduce(peak[:, 8 * t + 2 * g:8 * t + 2 * g + 2],
                                              bank[4 * t + g][:, :].rearrange("p (h s) -> p h s", s=S), AX.X, ALU.max)
                    chain(ins)
                    V.tensor_scalar(peak[:, 8 * t:8 * t + 8], peak[:, 8 * t:8 * t + 8], -AQK ** -0.5, None,
                                    ALU.mult).then_inc(ev("peak"), 1)
                dve.wait_ge(ev("prob"), 2 * l + 2)
                chain(V.reciprocal(ob_rstd, total))
                dve.wait_ge(ev("mla_o"), l + 1)
                a3 = lambda t: mix[:, t * 2 * D + D:t * 2 * D + D + 512].rearrange("p (h d) -> p h d", d=AV)
                for t in range(NT):
                    ins = tt(a3(t), bank[t][:, :].rearrange("p (h d) -> p h d", d=AV),
                             ob_rstd[:, 8 * t:8 * t + 8].unsqueeze(2).to_broadcast([P, AH, AV]), ALU.mult)
                ins.then_inc(ev("mla_y"), 1)
                dve.wait_ge(ev("mla_y"), l + 1)
                group_rms(ob_rstd, area(0, 1024).rearrange("p (n d) -> p n d", d=AV), 16, AV, 3)
                for t in range(NT):
                    ins = tt(a3(t), a3(t), ob_rstd[:, 8 * t:8 * t + 8].unsqueeze(2).to_broadcast([P, AH, AV]), ALU.mult)
                chain(ins)
                m5 = mix_part(D, 512, 2 * D)
                tt(m5, m5, lpar("mla_gain").unsqueeze(1).to_broadcast([P, NT, 512]), ALU.mult).then_inc(ev("mixed2"), 1)
                to_operand(10, None, 2 * KD, l)
                for i in range(8):
                    split(u0 + L_OUT + i + RING)
                residual(u0 + L_OUT + 7, 1.0)
                norm(2, lpar("ffn2_gain"), 18, l)
                ffn(u0 + L_FFN2, FFN_BLOCKS, blk + FFN_BLOCKS, False)
                split(u0 + L_UNITS + 2)
                residual(u0 + L_UNITS - 1, 0.5)

            for l in range(LAYERS):
                layer(l)
            dve.wait_ge(ev("x_ready"), at("x_ready", 0, LAYERS))
            V.memset(stats[:, 3:4], 0.0).then_inc(ev("result"), 1)

        @block.tensor
        def _(pe):
            mm, flip_of = nc.tensor.matmul, nc.tensor.transpose

            def three(o, a_hi, a_lo, b_hi, b_lo, start, stop_, shared=False):
                mm(o, a_lo, b_hi, start=start, stop=False, skip_group_check=shared)
                mm(o, a_hi, b_lo, start=False, stop=False, skip_group_check=shared)
                return mm(o, a_hi, b_hi, start=False, stop=stop_, skip_group_check=shared)

            def tokens(a, j, t):
                return a[:, j, t * P:(t + 1) * P]

            def tile_tm(n0, pair, width=512, units=2):
                for u in range(units):
                    n = n0 + u
                    s = n % RING
                    pe.wait_ge(lo_done, n + 1)
                    for t in range(NT):
                        for j in range(4):
                            c = slice(j * 512, j * 512 + width)
                            k = 4 * u + j
                            ins = three(bank[pair + t][:, 0:width], tokens(xh, k, t), tokens(xl, k, t),
                                        hi[s][:, c], lo[s][:, c], k == 0, k == 4 * units - 1)
                    ins.then_inc(consumed, 1)

            def tile_fm(n0, pair):
                for u in range(2):
                    n = n0 + u
                    s = n % RING
                    pe.wait_ge(lo_done, n + 1)
                    for f in range(4):
                        o = bank[pair + f // 2][:, (f % 2) * S:(f % 2 + 1) * S]
                        for j in range(4):
                            c = slice(j * 512 + f * P, j * 512 + (f + 1) * P)
                            k = 4 * u + j
                            ins = three(o, hi[s][:, c], lo[s][:, c], xh[:, k, :], xl[:, k, :],
                                        k == 0 and f % 2 == 0, k == 7, True)
                    ins.then_inc(consumed, 1)

            def three_small(o, k, t, c, start, stop_):
                return three(o, tokens(xh, k, t), tokens(xl, k, t), small_hi[:, c], small_lo[:, c], start, stop_)

            def to_operand(pairs, src, count, l=None):
                for j in range(0, count, 2):
                    if j >= 8:
                        pe.wait_ge(ev("xl_ready"), at("xl_ready", pairs + j // 2 - 3, l))
                    for jj in range(min(2, count - j)):
                        for t in range(NT):
                            ins = flip_of(bank[4 + (j // 2) % 4][:, jj * S + t * P:jj * S + (t + 1) * P], src(t, j + jj), ident)
                    ins.then_inc(ev("flip"), 1)

            def norm(k, pairs, l=None):
                pe.wait_ge(ev("normed"), at("normed", k + 1, l))
                to_operand(pairs, lambda t, j: mix[:, t * D + j * P:t * D + (j + 1) * P], KD, l)
                pe.wait_ge(ev("xl_ready"), at("xl_ready", pairs + 4, l))

            def out_product(n0, units_each):
                for c in range(2):
                    for u in range(units_each):
                        n = n0 + c * units_each + u
                        s = n % RING
                        pe.wait_ge(lo_done, n + 1)
                        for t in range(NT):
                            for j in range(4):
                                k = 4 * u + j
                                cc = slice(j * 512, (j + 1) * 512)
                                ins = three(bank[2 * t + c][:, :], tokens(xh, k, t), tokens(xl, k, t),
                                            hi[s][:, cc], lo[s][:, cc], k == 0, k == 4 * units_each - 1)
                        ins.then_inc(consumed, 1)

            def ffn(base, nb, blk0):
                def gate_up(b, n, slots, first):
                    for u, s in enumerate(slots):
                        pe.wait_ge(lo_done, n + u + 1)
                        if u == 0 and not first:
                            pe.wait_ge(ev("hid_ready"), b + blk0)
                        for t in range(NT):
                            for j in range(4):
                                k = 4 * u + j
                                c = slice(j * 512, (j + 1) * 512)
                                ins = three(bank[4 + t][:, :], tokens(xh, k, t), tokens(xl, k, t),
                                            hi[s][:, c], lo[s][:, c], k == 0, k == KD - 1)
                        ins.then_inc(consumed, 1)

                def down(b, n, s, first, last):
                    pe.wait_ge(lo_done, n + 1)
                    pe.wait_ge(ev("htl_ready"), b + blk0 + 1)
                    for f in range(2):
                        for t in range(NT):
                            for c in range(2):
                                cc = slice(f * D + c * 512, f * D + (c + 1) * 512)
                                ins = three(bank[2 * t + c][:, :], tokens(hth, f, t), tokens(htl, f, t),
                                            hi[s][:, cc], lo[s][:, cc], first and f == 0, last and f == 1, True)
                    ins.then_inc(consumed, 1)

                def hidden(b):
                    pe.wait_ge(ev("hid_ready"), b + blk0 + 1)
                    for f in range(2):
                        for t in range(NT):
                            ins = flip_of(bank[6][:, f * S + t * P:f * S + (t + 1) * P], hid[:, t, f * P:(f + 1) * P], ident)
                    ins.then_inc(ev("hid_flip"), 1)

                gate_up(0, base, [0, 1], True)
                hidden(0)

                def body(b, first=False):
                    gate_up(b, b * 3 + base - 1, [2, 0], False)
                    down(b - 1, b * 3 + base + 1, 1, first, False)
                    hidden(b)
                body(1, True)
                with pe.Fori(2, nb) as b:
                    body(b)
                down(nb - 1, base + 3 * nb - 1, 2, False, True)

            pe.wait_ge(ev("params_in"), 16)
            norm(0, 0)
            for c, (kind, pair) in enumerate([(tile_fm, 0), (tile_fm, 2), (tile_tm, 4), (tile_tm, 6),
                                              (tile_fm, 0), (tile_fm, 2), (tile_tm, 4)]):
                if c >= 4:
                    pe.wait_ge(ev("u_out"), c - 3)
                kind(2 * c, pair)
            pe.wait_ge(ev("small_lo"), 1)
            pe.wait_ge(ev("u_out"), 7)
            for t in range(NT):
                for k in range(KD):
                    ins = three_small(bank[6][:, t * FH:(t + 1) * FH], k, t, slice(k * 28, k * 28 + FH), k == 0, k == 7)
            ins.then_inc(ev("fox_f"), 1)
            for i in range(LEVELS + 2):
                if i == 0:
                    pe.wait_ge(ev("diff"), 1)
                else:
                    pe.wait_ge(ev("weighed"), i)
                if i >= 2:
                    pe.wait_ge(ev("kept"), i - 1)
                for g in range(8):
                    c = slice(g * P, (g + 1) * P)
                    src = decay[i % 2]
                    o = bank[2 * (i % 2) + g // 4][:, (g % 4) * P:(g % 4 + 1) * P]
                    if i == 0:
                        ins = mm(o, hk[:, c], hq[:, c], start=True, stop=True)
                    elif i <= LEVELS:
                        ins = mm(o, src[:, c], src[:, c], start=True, stop=True)
                    elif g < HH:
                        ins = mm(bank[2 * (i % 2)][:, g * P:(g + 1) * P], src[:, 2 * g * P:(2 * g + 1) * P],
                                 src[:, (2 * g + 1) * P:(2 * g + 2) * P], start=True, stop=True)
                ins.then_inc(ev("level"), 1)
            pe.wait_ge(ev("kept"), LEVELS + 2)
            for h in range(HH):
                c = slice(h * P, (h + 1) * P)
                v = [hv[:, t * 512 + h * P:t * 512 + (h + 1) * P] for t in range(NT)]
                mm(bank[4][:, c], score[:, 2 * h * P:(2 * h + 1) * P], v[0], start=True, stop=True)
                mm(bank[5][:, c], cross[:, c], v[0], start=True, stop=False)
                ins = mm(bank[5][:, c], score[:, (2 * h + 1) * P:(2 * h + 2) * P], v[1], start=False, stop=True)
            ins.then_inc(ev("hg_o"), 1)
            pe.wait_ge(ev("fox_log"), 1)
            for t in range(NT):
                ins = flip_of(bank[7][0:FH, t * P:(t + 1) * P], route[:, 32 + 8 * t:40 + 8 * t], ident)
            ins.then_inc(ev("fox_log_flip"), 1)
            pe.wait_ge(ev("fox_cum"), 1)
            for t in range(NT):
                w = P * (t + 1)
                for h in range(FH):
                    per = 512 // w
                    o = bank[2 * t + h // per][:, (h % per) * w:(h % per + 1) * w]
                    mm(o, fq[:, h * S + t * P:h * S + (t + 1) * P], fk[:, (h // 2) * S:(h // 2) * S + w],
                       start=True, stop=False)
                    ins = mm(o, ident[:, h:h + 1].to_broadcast([P, P]), fcum[:, 0:w], start=False, stop=True)
            ins.then_inc(ev("fox_logits"), 1)
            pe.wait_ge(ev("fox_exp"), 2)
            for g in range(6):
                for i in range(4):
                    q = 4 * g + i
                    src = logit[0][:, q * P:(q + 1) * P] if q < 8 else logit[1][:, (q - 8) * P:(q - 7) * P]
                    ins = flip_of(bank[g][:, i * P:(i + 1) * P], src, ident)
                ins.then_inc(ev("fox_flip"), 1)
            pe.wait_ge(ev("fox_pT"), 6)
            for h in range(FH):
                c = slice(h * FDH, (h + 1) * FDH)
                v = [fv[:, t * 512 + h * FDH:t * 512 + (h + 1) * FDH] for t in range(NT)]
                mm(bank[6][:, c], probT[:, h * P:(h + 1) * P], v[0], start=True, stop=True)
                mm(bank[7][:, c], probT[:, (8 + 2 * h) * P:(9 + 2 * h) * P], v[0], start=True, stop=False)
                ins = mm(bank[7][:, c], probT[:, (9 + 2 * h) * P:(10 + 2 * h) * P], v[1], start=False, stop=True)
            ins.then_inc(ev("fox_o"), 1)
            pe.wait_ge(ev("mixed"), 1)
            to_operand(4, lambda t, j: mix[:, t * D + j * P:t * D + (j + 1) * P], KD)
            pe.wait_ge(ev("xl_ready"), 8)
            out_product(U_OUT1, 2)
            norm(1, 8)
            for t in range(NT):
                for k in range(KD):
                    ins = three_small(bank[6][:, t * 20:(t + 1) * 20], k, t, slice(k * 28 + FH, (k + 1) * 28), k == 0, k == 7)
            ins.then_inc(ev("routed"), 1)
            ffn(U_MOE, MOE_BLOCKS, 0)

            def layer(l):
                u0 = U_LAYER + L_UNITS * l
                blk = MOE_BLOCKS + 2 * FFN_BLOCKS * l
                norm(0, 0, l)
                ffn(u0, FFN_BLOCKS, blk)
                norm(1, 4, l)
                for c in range(9):
                    pair = [0, 2, 4, 6, 0, 2, 4, 6, 0][c]
                    if c >= 4:
                        pe.wait_ge(ev("u_part"), 8 * l + [1, 2, 3, 4, 5][c - 4])
                    if c in (0, 1, 2, 4, 5):
                        tile_fm(u0 + L_IN + 2 * c, pair)
                    else:
                        tile_tm(u0 + L_IN + 2 * c, pair, 448 if c == 3 else 512)
                pe.wait_ge(ev("u_part"), 8 * l + 8)
                pe.wait_ge(ev("dt_a"), l + 1)
                for t in range(NT):
                    ins = flip_of(bank[7][0:32, t * P:(t + 1) * P], dt_a[:, 32 * t:32 * t + 32], ident)
                ins.then_inc(ev("dt_flip"), 1)
                pe.wait_ge(ev("conv3"), l + 1)
                for t in range(NT):
                    for i in range(CT):
                        ins = flip_of(bank[6 if t == 0 else 3][:, i * P:(i + 1) * P], c_in[:, i * S + t * P:i * S + (t + 1) * P], ident)
                ins.then_inc(ev("c_flip"), 1)
                pe.wait_ge(ev("rows"), l + 1)
                for t in range(NT):
                    ins = flip_of(bank[7][:, t * P:(t + 1) * P], rows[:, t * P:(t + 1) * P], ident)
                ins.then_inc(ev("rows_flip"), 1)
                pe.wait_ge(ev("xbc"), 3 * (l + 1))
                pe.wait_ge(ev("c_prod"), l + 1)
                pe.wait_ge(ev("conv_y"), l + 1)
                for t in range(NT):
                    for i in range(XC):
                        ins = flip_of(bank[2 * t + i // 4][:, (i % 4) * P:(i % 4 + 1) * P],
                                      xbc[:, i * S + t * P:i * S + (t + 1) * P], ident)
                ins.then_inc(ev("xs_flip"), 1)
                for g in range(SG):
                    for s in range(NT):
                        b_t = xbc[:, (8 + g) * S + s * P:(8 + g) * S + (s + 1) * P]
                        ins = mm(bank[4 + g][:, s * S:(s + 1) * S], b_t, xbc[:, (10 + g) * S:(11 + g) * S], start=True, stop=True)
                ins.then_inc(ev("cb"), 1)
                pe.wait_ge(ev("row_cols"), l + 1)
                pe.wait_ge(ev("xd"), l + 1)
                pe.wait_ge(ev("cb_out"), l + 1)
                future, past = par("future"), par("causal")[:, P:S]

                def exponents(h):
                    if h >= 2:
                        pe.wait_ge(ev("decays"), SH * l + h - 1)
                    b0, b1 = bank[2 * (h % 2)], bank[2 * (h % 2) + 1]
                    f_row = ident[:, h:h + 1].to_broadcast([P, P])
                    b_row = ident[:, SH + h:SH + h + 1].to_broadcast([P, P])
                    mm(b0[:, 0:256], f_row, rows[:, 0:S], start=True, stop=False)
                    mm(b0[:, 0:128], ident, future, start=False, stop=True)
                    mm(b0[:, 256:384], b_row, rows[:, 0:P], start=True, stop=False)
                    mm(b0[:, 256:384], ident, past, start=False, stop=True)
                    mm(b1[:, 0:256], b_row, rows[:, 0:S], start=True, stop=False)
                    mm(b1[:, 128:256], ident, past, start=False, stop=True)
                    mm(b1[:, 256:384], f_row, rows[:, P:S], start=True, stop=False)
                    mm(b1[:, 256:384], ident, future, start=False, stop=True).then_inc(ev("expo"), 1)

                exponents(0)
                for h in range(SH):
                    if h + 1 < SH:
                        exponents(h + 1)
                    pe.wait_ge(ev("scores"), SH * l + h + 1)
                    e = expo[h % 2]
                    c = slice((h % 8) * SP_, (h % 8 + 1) * SP_)
                    xf = [xd_f[:, t * D + h * SP_:t * D + (h + 1) * SP_] for t in range(NT)]
                    xb = [mix[:, t * 2 * D + D + h * SP_:t * 2 * D + D + (h + 1) * SP_] for t in range(NT)]
                    y0, y1 = bank[4 + h // 8][:, c], bank[6 + h // 8][:, c]
                    mm(y0, e[:, 0:128], xf[0], start=True, stop=False)
                    mm(y0, e[:, 256:384], xb[0], start=False, stop=False)
                    mm(y0, e[:, 384:512], xb[1], start=False, stop=True)
                    mm(y1, e[:, 128:256], xf[0], start=True, stop=False)
                    mm(y1, e[:, 640:768], xf[1], start=False, stop=False)
                    mm(y1, e[:, 512:640], xb[1], start=False, stop=True).then_inc(ev("y_head"), 1)
                pe.wait_ge(ev("lat"), l + 1)
                to_operand(8, lambda t, j: misc[:, t, 32 + j * P:32 + (j + 1) * P], 3, l)
                pe.wait_ge(ev("xl_ready"), at("xl_ready", 10, l))
                n = u0 + L_MLA
                s = n % RING
                pe.wait_ge(lo_done, n + 1)
                for t in range(NT):
                    for a, w in [(0, 512), (512, 256)]:
                        for k in range(2):
                            c = slice(k * 768 + a, k * 768 + a + w)
                            three(bank[2 * t + a // 512][:, 0:w], tokens(xh, k, t), tokens(xl, k, t),
                                  hi[s][:, c], lo[s][:, c], k == 0, k == 1)
                    ins = three(bank[4 + t][:, :], tokens(xh, 2, t), tokens(xl, 2, t), hi[s][:, 1536:], lo[s][:, 1536:], True, True)
                ins.then_inc(consumed, 1)
                pe.wait_ge(ev("ukv_lo"), l + 1)
                for t in range(NT):
                    ins = three(bank[6 + t][:, :], tokens(xh, 2, t), tokens(xl, 2, t), small_hi[:, :], small_lo[:, :], True, True)
                ins.then_inc(ev("kv_done"), 1)
                pe.wait_ge(ev("qk"), l + 1)
                for g in range(8):
                    for h in range(2):
                        for t in range(NT):
                            a = (g // 4) * 1536 + t * 768 + (2 * (g % 4) + h) * AQK
                            ins = flip_of(bank[g][0:AQK, h * S + t * P:h * S + (t + 1) * P], qk[:, a:a + AQK], ident)
                    ins.then_inc(ev("qk_flip"), 1)
                pe.wait_ge(ev("qk_t"), 8 * (l + 1))
                for t in range(NT):
                    for h in range(AH):
                        ins = mm(bank[4 * t + h // 2][:, (h % 2) * S:(h % 2 + 1) * S],
                                 q_t[0:AQK, h * S + t * P:h * S + (t + 1) * P], k_t[0:AQK, h * S:(h + 1) * S], start=True, stop=True)
                    ins.then_inc(ev("logits"), 1)
                for g in range(8):
                    if g % 4 == 0:
                        pe.wait_ge(ev("prob"), 2 * l + g // 4 + 1)
                    for i in range(4):
                        ins = flip_of(bank[g][:, i * P:(i + 1) * P], prob[g // 4][:, (4 * (g % 4) + i) * P:(4 * (g % 4) + i + 1) * P], ident)
                    ins.then_inc(ev("prob_flip"), 1)
                pe.wait_ge(ev("prob_t"), 8 * (l + 1))
                for t in range(NT):
                    for h in range(AH):
                        for s in range(NT):
                            ins = mm(bank[t][:, h * AV:(h + 1) * AV], prob_t[t][:, (2 * h + s) * P:(2 * h + s + 1) * P],
                                     va[:, s * 512 + h * AV:s * 512 + (h + 1) * AV], start=s == 0, stop=s == 1)
                ins.then_inc(ev("mla_o"), 1)
                pe.wait_ge(ev("mixed2"), l + 1)
                to_operand(10, lambda t, j: mix[:, t * 2 * D + j * P:t * 2 * D + (j + 1) * P], 2 * KD, l)
                pe.wait_ge(ev("xl_ready"), at("xl_ready", 18, l))
                out_product(u0 + L_OUT, 4)
                norm(2, 18, l)
                ffn(u0 + L_FFN2, FFN_BLOCKS, blk + FFN_BLOCKS)

            if stop is None:
                for l in range(LAYERS):
                    layer(l)


def columns(w, c, width=512):
    k = w.shape[0]
    part = np.zeros((k, 512), w.dtype)
    part[:, :width] = w[:, c:c + width]
    return part.reshape(k // 512, 4, P, 512).transpose(0, 2, 1, 3).reshape(k // 512, P, UNIT)


def swiglu_units(gate, up, down):
    nb = gate.shape[1] // BLK

    def gate_up(b):
        c = slice(b * BLK, (b + 1) * BLK)
        return list(columns(np.concatenate([gate[:, c], up[:, c]], axis=1), 0))

    def rows(b):
        return [down[b * BLK:(b + 1) * BLK].reshape(2, P, D).transpose(1, 0, 2).reshape(P, UNIT)]

    units = gate_up(0)
    for b in range(1, nb):
        units += gate_up(b) + rows(b - 1)
    return units + rows(nb - 1)


def across(row):
    return np.broadcast_to(np.asarray(row).reshape(1, -1), (P, np.asarray(row).size))


def down_columns(v):
    return np.asarray(v).reshape(-1, P).T


def table(spec, values):
    out = np.zeros((P, sum(w for _, w in spec)), np.float32)
    at = 0
    for name, width in spec:
        out[:, at:at + width] = values[name]
        at += width
    return out


def constants():
    p = np.arange(P)
    half = np.zeros((P, 2), np.float32)
    half[:64, 0] = half[64:, 1] = 0.125
    sign, back = np.ones((P, 1), np.float32), np.zeros((P, 1), np.float32)
    sign[SH:2 * SH], back[SH:2 * SH] = -1.0, 1.0
    freq = 10000.0 ** (-np.arange(ROPE // 2, dtype=np.float32) / np.float32(ROPE // 2))
    return {
        "ident": np.eye(P, dtype=np.float32),
        "causal": np.concatenate([np.zeros((P, P)), np.where(p[:, None] >= p[None, :], 0.0, -BIG)], axis=1),
        "future": np.where(p[:, None] <= p[None, :], 0.0, -BIG).astype(np.float32),
        "half_scale": half, "desc4": across(np.array([4, 3, 2, 1], np.float32)),
        "row_sign": sign, "row_back": back, "inv_freq": across(freq.astype(np.float32)),
    }


def level_masks():
    s, t = np.arange(P)[:, None], np.arange(P)[None, :]
    out = [s == t]
    for i in range(1, LEVELS + 1):
        w = 1 << (i - 1)
        out.append((s // (2 * w) == t // (2 * w)) & (s % (2 * w) < w) & (t % (2 * w) >= w))
    return np.stack(out, axis=1).astype(np.float32).reshape(P, -1)


def kernel(**inputs):
    import concourse.bacc as bacc
    from concourse.bass_utils import run_bass_kernel_spmd

    a = {k: np.asarray(v) for k, v in inputs.items()}
    units = []
    for c in range(7):
        units += list(columns(a["w_in"][0], c * 512))
    for c in range(2):
        units += list(columns(a["w_out"][0], c * 512))
    gate, up, down = a["w_gate"][0], a["w_up"][0], a["w_down"][0]
    units += swiglu_units(gate.transpose(1, 0, 2).reshape(D, NE * EF), up.transpose(1, 0, 2).reshape(D, NE * EF),
                          down.reshape(NE * EF, D))
    lp = []
    for l in range(LAYERS):
        units += swiglu_units(a["ffn1_w_gate_2"][l], a["ffn1_w_up_2"][l], a["ffn1_w_down_2"][l])
        w = a["w_in_2"][l]
        cols = layer_columns()
        for c, width in cols:
            units += list(columns(w, c, width))
        uq = a["mla_w_uq_2"][l].reshape(2, P, AH * AQK).transpose(1, 0, 2).reshape(P, -1)
        ukv = a["mla_w_ukv_2"][l]
        units.append(np.concatenate([uq, ukv[:, :512]], axis=1))
        for c in range(2):
            units += list(columns(a["w_out_2"][l], c * 512))
        units += swiglu_units(a["ffn2_w_gate_2"][l], a["ffn2_w_up_2"][l], a["ffn2_w_down_2"][l])
        cw5, cw3 = a["ssd_conv_w_2"][l], a["conv_w_2"][l]
        lp.append(table(LAYER_PARAMS, {
            "ffn1_gain": down_columns(a["ffn1_norm_2"][l]), "mix_gain": down_columns(a["mix_norm_2"][l]),
            "ffn2_gain": down_columns(a["ffn2_norm_2"][l]),
            "conv5_w": cw5.reshape(5, XT, P).transpose(2, 1, 0).reshape(P, -1),
            "conv5_b": down_columns(a["ssd_conv_b_2"][l]),
            "dt_bias": across(a["ssd_dt_bias_2"][l]), "a_log": across(a["ssd_a_log_2"][l]),
            "d_skip": across(a["ssd_d_2"][l]), "ssd_gain": across(a["ssd_norm_2"][l]),
            "q_gain": down_columns(a["mla_q_norm_2"][l]), "kv_gain": down_columns(a["mla_kv_norm_2"][l]),
            "qh_gain": across(a["mla_q_head_norm_2"][l]), "kh_gain": across(a["mla_k_head_norm_2"][l]),
            "mla_gain": across(a["mla_out_norm_2"][l]),
            "conv3_w": cw3.reshape(3, CT, P).transpose(2, 1, 0).reshape(P, -1),
            "conv_gain": across(a["conv_out_norm_2"][l]), "ukv_w": a["mla_w_ukv_2"][l][:, 512:],
        }))
    assert len(units) == N_UNITS
    small = np.concatenate([a["w_in"][0][:, 7 * 512:], a["w_group"][0], a["w_expert"][0]], axis=1)
    prm = table(PARAMS, {
        **constants(), "attn_gain": down_columns(a["attn_norm"][0]), "ffn_gain": down_columns(a["ffn_norm"][0]),
        "lb_logits": a["hg_lb_logits"].reshape(2, HH, P).transpose(2, 0, 1).reshape(P, -1),
        "hg_gain": across(a["hg_norm"][0]), "fox_gain": across(a["fox_norm"][0]), "fox_bias": across(a["fox_f_bias"][0]),
        "router_bias": across(np.concatenate([a["b_group"][0], a["b_expert"][0]])),
        "small_w": small.reshape(KD, P, -1).transpose(1, 0, 2).reshape(P, -1),
    })
    arrays = {
        "stream": np.stack(units), "x_in": a["x"][0],
        "positions": np.ascontiguousarray(a["positions_2"].reshape(NT, P).T), "params": prm,
        "level_masks": level_masks(), "final_gain": a["final_norm"].reshape(1, D), "layer_params": np.stack(lp),
    }
    nc = bacc.Bacc("TRN2", target_bir_lowering=False, num_devices=1)
    aps = [nc.dram_tensor(n, v.shape, mybir.dt.from_np(v.dtype), kind="ExternalInput").ap() for n, v in arrays.items()]
    out = nc.dram_tensor("out", (S, D), F32, kind="ExternalOutput").ap()
    two_blocks(nc, *aps, out, **STOP)
    got = run_bass_kernel_spmd(nc, [arrays], core_ids=[0]).results[0]["out"]
    return got.reshape(1, S, D)


STOP = {}


def layer_columns():
    xbc, dt, conv = SH * SP_, SH * SP_ + XT * P, SH * SP_ + XT * P + 448
    return ([(xbc + 512 * i, 512) for i in range(3)] + [(dt, 448)] + [(conv, 512), (conv + 1024, 512)]
            + [(conv + 512, 512)] + [(512 * i, 512) for i in range(2)])
```

```python
from contextlib import ExitStack

import numpy as np

import concourse.bass as bass
from concourse import mybir

F32 = mybir.dt.float32
F32R = mybir.dt.float32r
U32 = mybir.dt.uint32
I32 = mybir.dt.int32
ALU = mybir.AluOpType
ACT = mybir.ActivationFunctionType
AX = mybir.AxisListType

P = 128
S = 256
NT = S // P
D = 1024
KD = D // P
UNIT = 2048
RING = 3
EPS = 1e-6
BIG = 1e30

HH, HDK = 4, 128
FH, FDH = 8, 64
NG, NE = 4, 16
EF = 512
BLK = 256
MOE_BLOCKS = NE * EF // BLK
LEVELS = 7

LAYERS = 2
DFF = 2816
FFN_BLOCKS = DFF // BLK
SH, SP_, SG, SN = 16, 64, 2, 128
XT = 12
XC = 8
AH, AQK, AV, NOPE, ROPE = 8, 96, 64, 64, 32
QL, KVL = 256, 128
CT = 4

U_IN1 = 0
U_OUT1 = U_IN1 + 7 * 2
U_MOE = U_OUT1 + 4
U_LAYER = U_MOE + 3 * MOE_BLOCKS
L_FFN1 = 0
L_IN = L_FFN1 + 3 * FFN_BLOCKS
L_OUT = L_IN + 9 * 2 + 1
L_FFN2 = L_OUT + 8
L_UNITS = L_FFN2 + 3 * FFN_BLOCKS
N_UNITS = U_LAYER + LAYERS * L_UNITS

PARAMS = [
    ("causal", 2 * P),
    ("half_scale", 2), ("desc4", 4), ("inv_freq", ROPE // 2),
    ("attn_gain", KD), ("ffn_gain", KD), ("lb_logits", 2 * HH), ("hg_gain", HDK), ("fox_gain", FDH),
    ("fox_bias", 1), ("router_bias", NG + NE), ("small_w", KD * (FH + NG + NE)),
]
LAYER_PARAMS = [
    ("ffn1_gain", KD), ("mix_gain", KD), ("ffn2_gain", KD), ("conv5_w", XT * 5), ("conv5_b", XT),
    ("dt_bias", 2 * SH), ("a_log", 2 * SH), ("d_skip", SH), ("ssd_gain", D), ("q_gain", 2), ("kv_gain", 1),
    ("qh_rows", 1), ("kh_rows", 1), ("qh_rope", ROPE), ("kh_rope", ROPE), ("mla_gain", AH * AV), ("conv3_w", CT * 3), ("conv_gain", 512),
]


def offsets(table):
    at, out = 0, {}
    for name, width in table:
        out[name] = (at, width)
        at += width
    return out, at


P_AT, P_COLS = offsets(PARAMS)
LP_AT, LP_COLS = offsets(LAYER_PARAMS)


ROUND = 12582912.0
TURN = 2 * np.pi
TURN_HI = 6.28125
TURN_LO = TURN - TURN_HI
PI_BELOW = 3.1415925
SMALL = KD * (FH + NG + NE)
ARENA = 13312
KV_BANK = [7, 2, 4, 5]

IN1_TILES = [1, 0, 2, 3, 4, 5, 6]
IN1_PAIR = [0, 2, 4, 6, 4, 6, 4]

MLA_AT = 4
IN_UNITS = [(c, u) for c in range(9) for u in range(2)]
IN_UNITS.insert(MLA_AT, (None, 0))
FEATURE_MAJOR = (1, 2, 3, 4, 5)
STEPS = {
    2: ["latents"], 4: ["taps_1"], 6: ["keys_values", "silu_1", "taps_2"], 7: ["head_sums"],
    8: ["silu_2", "rotate"], 9: ["taps_3"], 10: ["flip_q", "flip_k", "attend_0"], 11: ["silu_3"],
    12: ["weights_0"], 13: ["weigh_0"], 14: ["attend_1"], 15: ["weights_1", "weigh_1", "rates", "values"],
    16: ["xs"], 17: ["cb", "early_0"], 18: ["head_0", "head_1"],
}

HEADS_BEFORE = sum(name.startswith("head_") and name != "head_sums" for names in STEPS.values() for name in names)

MIX_TILES = list(range(8, 16)) + list(range(8))
MIX_BANK = [0, 1, 2, 3, 1, 3, 4, 5]
GATE_AFTER, SQUARES_AFTER, NORM_AFTER = 8, 9, 12
FLIP_AFTER = {8: [0, 1], 9: [2, 3], 13: [4, 5]}
TAKE_AFTER = {10: [0, 1], 11: [2, 3]}

COUNTS = {
    "x_ready": (3, 3), "norm_root": (3, 3), "normed": (1, 1), "rstd": (1, 2), "y_half": (1, 2), "x_half": (2, 3), "flip": (12, 22), "xh_ready": (12, 22),
    "xl_ready": (12, 22), "sq": (2, 2), "sq_sum": (2, 2), "root": (2, 2),
}


def two_blocks(nc, stream, x_in, positions, prm_in, mask_in, array_in, final_in, ukv_in, lprm_in, out):
    with ExitStack() as ctx:
        def sb(name, shape, dt=F32):
            return ctx.enter_context(nc.sbuf_tensor(name, shape, dt))

        sems = {}

        def ev(name):
            if name not in sems:
                sems[name] = ctx.enter_context(nc.semaphore(name))
            return sems[name]

        def at(name, k, l=None):
            before, each = COUNTS.get(name, (0, 1))
            return k if l is None else before + each * l + k

        raw = [sb(f"raw{i}", [P, UNIT]) for i in range(RING)]
        hi = [sb(f"hi{i}", [P, UNIT], F32R) for i in range(RING)]
        lo = [sb(f"lo{i}", [P, UNIT], F32R) for i in range(RING)]
        xh = sb("xh", [P, 2 * KD, S], F32R)
        xl = sb("xl", [P, 2 * KD, S], F32R)
        x = sb("x", [P, NT, D])
        mix = sb("mix", [P, NT * 2 * D])
        prm = sb("prm", [P, P_COLS])
        lprm = sb("lprm", [P, LP_COLS])
        array = sb("array", [P, 3 * P], F32R)
        small_hi = sb("small_hi", [P, 512], F32R)
        small_lo = sb("small_lo", [P, 512], F32R)
        rows_hi, rows_lo, rows_both = small_hi[0:SH, :], small_hi[32:32 + SH, :], small_hi[0:32 + SH, :]
        pick = sb("pick", [P, SH], F32R)
        stats = sb("stats", [P, 64])
        hth = sb("hth", [P, 2, S], F32R)
        htl = sb("htl", [P, 2, S], F32R)
        gates = sb("gates", [P, NT, NE, 2])
        route = sb("route", [P, 640])
        trig = sb("trig", [P, 2 * NT * ROPE // 2])
        pos = sb("pos", [P, NT], I32)
        turns_by = [sb(f"turns_{n}", [P, 2, NT, ROPE // 2]) for n in ("cos_first", "sin_second", "sin_first", "cos_second")]
        arena = sb("arena", [P, ARENA])
        bank = [ctx.enter_context(nc.psum_tensor(f"bank{i}", [P, 512], F32)) for i in range(8)]

        def par(name):
            a, width = P_AT[name]
            return prm[:, a:a + width]

        def lpar(name):
            a, width = LP_AT[name]
            return lprm[:, a:a + width]

        def mix_part(a, width, row):
            return mix[:, 0:NT * row].rearrange("p (t d) -> p t d", d=row)[:, :, a:a + width]

        def area(a, width):
            assert a + width <= ARENA
            return arena[:, a:a + width]

        sil = mix[:, 0:NT * BLK].rearrange("p (t f) -> p t f", t=NT)
        hid = mix[:, NT * BLK:2 * NT * BLK].rearrange("p (t f) -> p t f", t=NT)
        ident_r, ident = array[:, 0:P], array[:, 0:P].bitcast(F32)
        future, past = array[:, P:2 * P].bitcast(F32), array[:, 2 * P:3 * P].bitcast(F32)
        eps_col, one_col = stats[:, 0:1], stats[:, 1:2]
        sumsq, root, rstd = stats[:, 8:10], stats[:, 10:12], stats[:, 12:14]

        hq, hk, hb = area(0, 1024), area(1024, 1024), area(2048, 1024)
        decay = [area(3072, 1024), area(4096, 1024)]
        score, cross = area(5120, 1024), area(6144, 512)
        hv, hg = area(6656, 1024), area(7680, 1024)
        fk, fv = area(8704, 1024), area(9728, 1024)
        level_mask, restart = area(10752, 1024), area(11776, 1024)
        fq = mix[:, 2048:4096]
        logit = [area(0, 1024), area(1024, 2048)]
        probT = area(3072, 3072)
        fcum, flog = area(12800, 256), area(13056, 256)
        fcum_hi, fcum_lo, fcum_both = hth[0:32, 0, :], hth[32:64, 0, :], hth[0:64, 0, :]

        final_gain = area(0, D)
        array_raw = area(12800, 3 * P)

        qk, qk_sq = area(0, 3072), area(3072, 3072)
        prob, prob_t = area(0, 2048), area(7168, 2048)
        q_t, k_t = area(3072, 2048), area(5120, 2048)
        misc = area(7168, 896).rearrange("p (t n) -> p t n", t=NT)
        ukv_raw = area(8064, 512)
        va = area(9216, 1024)
        xbc = area(10240, XT * S)
        xs, cb_score, zs = area(0, 2048), area(2048, 2 * 768), area(3584, 2048)
        expo = [area(5632, 768), area(6400, 768), area(12288, 768)]
        rows, rate, cum = area(5632, 2 * S), area(6144, 2 * S), area(6656, 2 * S)
        skip = area(10240, 2048)
        conv_buf = [mix[:, 0:D], mix[:, 2 * D:3 * D]]
        gains_q = lprm[:, LP_AT["q_gain"][0]:LP_AT["q_gain"][0] + 3]
        dt, dt_tmp, dt_a = route[:, 0:64], route[:, 64:128], route[:, 128:192]
        row_columns = route[:, 432:496]
        a_exp = route[:, 256:288]
        qk_sum, qk_root, qk_rstd = route[:, 288:320], route[:, 320:352], route[:, 352:384]
        peak, total = route[:, 384:400], route[:, 400:416]
        ob_rstd = route[:, 416:432]
        q_scale = route[:, 496:512]

        def spans(h):
            return [(slice(0, 256), slice(0, S), slice(h, h + 1), slice(h, h + 1)),
                    (slice(256, 512), slice(S, 2 * S), slice(48 + h, 49 + h), slice(48 + h, 49 + h)),
                    (slice(512, 640), slice(S, S + P), slice(32 + h, 33 + h), slice(16 + h, 17 + h)),
                    (slice(640, 768), slice(P, S), slice(16 + h, 17 + h), slice(32 + h, 33 + h))]

        raw_in = [ev(f"raw_in{i}") for i in range(RING)]
        hi_done, lo_done, consumed = ev("hi_done"), ev("lo_done"), ev("consumed")

        class Chain:

            def __init__(self, eng, name):
                self.eng, self.sem, self.n = eng, ev(name), 0

            def __call__(self, ins):
                ins.then_inc(self.sem, 1)
                self.n += 1
                self.eng.wait_ge(self.sem, self.n)

        block = ctx.enter_context(nc.Block())

        @block.sync
        def _(sp):
            sp.dma_start(x[:, :, :], x_in.rearrange("(t p) d -> p t d", p=P)).then_inc(ev("x_in"), 16)
            sp.dma_start(array_raw, array_in).then_inc(ev("array_in"), 16)
            sp.dma_start(prm[:, :], prm_in).then_inc(ev("params_in"), 16)
            for n in range(RING):
                sp.dma_start(raw[n][:, :], stream[n]).then_inc(raw_in[n], 16)
            sp.dma_start(level_mask, mask_in).then_inc(ev("mask_in"), 16)
            sp.dma_start(pos[:, :], positions).then_inc(ev("pos_in"), 16)
            sp.dma_start(lprm[:, :], lprm_in[0]).then_inc(ev("lprm_in"), 16)
            with sp.Fori(1, N_UNITS // RING) as g:
                for s in range(RING):
                    sp.wait_ge(lo_done, (g - 1) * RING + s + 1)
                    sp.dma_start(raw[s][:, :],
                                 stream[bass.ds(g * RING + s, 1)].rearrange("o p n -> (o p) n")
                                 ).then_inc(raw_in[s], 16)
            sp.wait_ge(ev("result"), 1)
            sp.dma_start(out.rearrange("(t p) d -> p t d", p=P), x[:, :, :]).then_inc(ev("stored"), 16)
            sp.wait_ge(ev("stored"), 16)

        @block.scalar
        def _(act):
            chain = Chain(act, "act_chain")
            A = nc.scalar.activation

            def split_at(n, slot, group):
                act.wait_ge(raw_in[slot], (group + 1) * 16)
                if not isinstance(n, int) or n >= RING:
                    act.wait_ge(consumed, n - RING + 1)
                A(hi[slot][:, :], raw[slot][:, :], ACT.Copy).then_inc(hi_done, 1)

            def split(n):
                if n < N_UNITS:
                    split_at(n, n % RING, n // RING)

            def root_of(tag, ncols, width, l=None):
                act.wait_ge(ev("sq_sum"), at("sq_sum", tag, l))
                A(stats[:, 32:32 + ncols], stats[:, 16:16 + ncols], ACT.Sqrt, scale=1.0 / width,
                  bias=eps_col).then_inc(ev("root"), 1)

            def norm(k, gain, pairs, l=None):
                row_norm(k, l)
                to_operand(pairs, gain, KD, l)

            def late_norm(k, gain, pairs, unit, l=None):
                to_operand(pairs, gain, KD, l)
                split(unit)
                row_norm(k, l)

            def row_norm(k, l=None):
                A(stats[:, 14:15], one_col, ACT.Sqrt)
                if k or l is not None:
                    act.wait_ge(ev("x_ready"), at("x_ready", k, l))
                for t in range(NT):
                    ins = A(mix[:, t * D:(t + 1) * D], x[:, t, :], ACT.Square, accum_out=sumsq[:, t:t + 1])
                chain(ins)
                A(root, sumsq, ACT.Sqrt, scale=1.0 / D, bias=eps_col).then_inc(ev("norm_root"), 1)

            def to_operand(pairs, gain, count, l=None, first=0, begin=0):
                for j in range(begin, count):
                    if j % 2 == 0:
                        act.wait_ge(ev("flip"), at("flip", pairs + j // 2 + 1, l))
                    src = bank[4 + (j // 2) % 4]
                    if gain is None:
                        if j % 2 == 0:
                            A(xh[:, j:j + 2, :], src[:, :], ACT.Copy).then_inc(ev("xh_ready"), 1)
                        continue
                    ins = A(xh[:, first + j, :], src[:, (j % 2) * S:(j % 2 + 1) * S], ACT.Copy, scale=gain[:, j:j + 1])
                    if j % 2 or j == count - 1:
                        ins.then_inc(ev("xh_ready"), 1)

            def ffn(base, g0, nb, blk0, norm_at):
                def silu(b):
                    for t in range(NT):
                        ins = A(sil[:, t, :], bank[4 + t][:, 0:BLK], ACT.Silu, scale=rstd[:, t:t + 1])
                    ins.then_inc(ev("silu"), 1)

                def hidden(b):
                    act.wait_ge(ev("hid_flip"), b + blk0 + 1)
                    A(hth[:, :, :], bank[6][:, :], ACT.Copy).then_inc(ev("hth_ready"), 1)

                split_at(base + 3, 0, g0 + 1)
                act.wait_ge(consumed, base + 2)
                act.wait_ge(ev("rstd"), norm_at)
                silu(0)
                split_at(base + 4, 1, g0 + 1)
                hidden(0)

                def body(b):
                    split_at(b * 3 + base + 2, 2, b + g0)
                    act.wait_ge(consumed, b * 3 + base + 1)
                    silu(b)
                    split_at(b * 3 + base + 3, 0, b + g0 + 1)
                    split_at(b * 3 + base + 4, 1, b + g0 + 1)
                    hidden(b)
                body(1)
                with act.Fori(2, nb - 1) as b:
                    body(b)
                split(base + 3 * nb - 1)
                act.wait_ge(consumed, base + 3 * nb - 2)
                silu(nb - 1)
                hidden(nb - 1)
                split(base + 3 * nb)
                split(base + 3 * nb + 1)

            act.wait_ge(ev("consts"), 1)
            act.wait_ge(ev("x_in"), 16)
            row_norm(0)
            act.wait_ge(ev("array_in"), 16)
            A(array[:, :], array_raw, ACT.Copy).then_inc(ev("array"), 1)
            act.wait_ge(ev("params_in"), 16)
            A(small_hi[:, 0:SMALL], par("small_w"), ACT.Copy).then_inc(ev("small_hi"), 1)
            split(0)
            to_operand(0, par("attn_gain"), KD)
            split(1)
            split(2)
            act.wait_ge(ev("lb_diff"), 1)
            A(stats[:, 48:52], stats[:, 4:8], ACT.Sigmoid).then_inc(ev("lb"), 1)

            def tile_out1(i):
                c = IN1_TILES[i]
                act.wait_ge(consumed, 2 * i + 2)
                for j in range(2):
                    src = bank[IN1_PAIR[i] + j]
                    if c == 4:
                        for half in range(2):
                            dst = fq.rearrange("p (j h t) -> p j h t", h=2, t=S)[:, 2 * j:2 * j + 2, half, :]
                            ins = A(dst, src[:, :].rearrange("p (j t) -> p j t", t=S), ACT.Copy,
                                    scale=par("half_scale")[:, half:half + 1])
                        continue
                    dst, func = [(hq, ACT.Silu), (decay[0], ACT.Sigmoid), (hv, ACT.Copy), (hg, ACT.Silu),
                                 None, (fk, ACT.Copy), (fv, ACT.Copy)][c]
                    ins = A(dst[:, j * 512:(j + 1) * 512], src[:, :], func)
                ins.then_inc(ev("u_out"), 1)

            for m in range(14):
                split(m + RING)
                if m % 2:
                    tile_out1(m // 2)
                if m == 0:
                    act.wait_ge(ev("trig_arg"), 1)
                    A(trig[:, :], trig[:, :], ACT.Sin).then_inc(ev("trig"), 1)
                if m == 2:
                    act.wait_ge(ev("f_ready"), 1)
                    A(decay[0], decay[1], ACT.Ln).then_inc(ev("log_f"), 1)
                    f_tmp = route[0:FH, 256:512]
                    act.wait_ge(ev("fox_x"), 1)
                    chain(A(f_tmp, route[0:FH, 0:256], ACT.Abs))
                    chain(A(f_tmp, f_tmp, ACT.Exp, scale=-1.0))
                    A(f_tmp, f_tmp, ACT.Ln, bias=one_col[0:FH, :]).then_inc(ev("fox_ln"), 1)
                if m == 3:
                    act.wait_ge(ev("fox_cum"), 1)
                    A(fcum_hi, fcum[0:32, :], ACT.Copy).then_inc(ev("fox_cum_hi"), 1)
                if m == 4 or 6 <= m <= 12:
                    i = max(1, m - 4)
                    act.wait_ge(ev("diff"), i)
                    A(decay[i % 2], decay[i % 2], ACT.Exp).then_inc(ev("decay"), 1)
            act.wait_ge(ev("hg_o"), 1)
            for t in range(NT):
                ins = A(hv[:, t * 512:(t + 1) * 512], bank[6 + t][:, :], ACT.Square)
            ins.then_inc(ev("sq"), 1)
            for t in range(NT):
                w = P * (t + 1)
                act.wait_ge(ev("fox_peak"), t + 1)
                for h in range(FH):
                    i = FH * t + h
                    ins = A(logit[t][:, h * w:(h + 1) * w], logit[t][:, h * w:(h + 1) * w], ACT.Exp,
                            bias=route[:, 64 + i:65 + i], accum_out=route[:, 80 + i:81 + i])
                ins.then_inc(ev("fox_exp"), 1)
            root_of(1, NT * HH, HDK)
            for g in range(6):
                act.wait_ge(ev("fox_flip"), g + 1)
                A(probT[:, g * 512:(g + 1) * 512], bank[g][:, :], ACT.Copy).then_inc(ev("fox_pT"), 1)
            to_operand(4, None, 4)
            act.wait_ge(ev("fox_norm"), 1)
            A(logit[0].rearrange("p (t d) -> p t d", t=NT), mix_part(512, 512, D), ACT.Square).then_inc(ev("sq"), 1)
            root_of(2, NT * FH, FDH)
            to_operand(4, None, KD, begin=4)
            for i in range(3):
                split(U_OUT1 + i + RING)
            late_norm(1, par("ffn_gain"), 8, U_MOE + 2)
            act.dma_start(final_gain, final_in.to_broadcast([P, D])).then_inc(ev("final_in"), 16)
            act.wait_ge(ev("route_g"), 1)
            A(route[:, 48:56], route[:, 40:48], ACT.Exp).then_inc(ev("route_ge"), 1)
            act.wait_ge(ev("route_e"), 1)
            A(route[:, 120:122], route[:, 118:120], ACT.Exp).then_inc(ev("route_ee"), 1)
            ffn(U_MOE, U_MOE // RING, MOE_BLOCKS, 0, 1)
            row_norm(2)

            def layer(l):
                u0 = U_LAYER + L_UNITS * l
                blk = MOE_BLOCKS + 2 * FFN_BLOCKS * l
                act.wait_ge(ev("x_ready"), at("x_ready", 0, l))
                act.dma_start(ukv_raw, ukv_in[l]).then_inc(ev("ukv_in"), 16)
                act.wait_ge(ev("lprm_in"), 16 * (l + 1))
                late_norm(0, lpar("ffn1_gain"), 0, u0 + 2, l)
                ffn(u0, u0 // RING, FFN_BLOCKS, blk, at("rstd", 1, l))
                act.wait_ge(ev("ukv_in"), 16 * (l + 1))
                A(small_hi[:, :], ukv_raw, ACT.Copy).then_inc(ev("ukv_hi"), 1)
                row_norm(1, l)
                split(u0 + L_IN + 2)
                to_operand(4, lpar("mix_gain"), KD, l)

                def tile_out(c):
                    pair = 2 * (c % 2)
                    for i in range(2):
                        src = bank[pair + i]
                        if c == 0:
                            ins = A(misc[:, i, :], src[:, 0:448], ACT.Copy)
                        elif c <= 4:
                            ins = A(conv_buf[(c + 1) % 2][:, i * 512:(i + 1) * 512], src[:, :], ACT.Copy)
                            for j in range(2 * i, 2 * i + 2 if c < 4 else 0):
                                k = (4 * c - 4 + j) * 5 + 2
                                ins = A(xbc[:, (4 * c - 4 + j) * S:(4 * c - 3 + j) * S], src[:, (j % 2) * S:(j % 2 + 1) * S],
                                        ACT.Copy, scale=lpar("conv5_w")[:, k:k + 1])
                        elif c == 6:
                            ins = A(mix[:, i * 2 * D + 1536:(i + 1) * 2 * D], src[:, :], ACT.Copy)
                        else:
                            ins = A(zs[:, i * D + (c - 7) * 512:i * D + (c - 6) * 512], src[:, :], ACT.Silu)
                    ins.then_inc(ev("u_part"), 1)

                def xbc_silu(c):
                    act.wait_ge(ev("conv5"), 3 * l + c)
                    for i in range(4 * c - 4, 4 * c):
                        ins = A(xbc[:, i * S:(i + 1) * S], xbc[:, i * S:(i + 1) * S], ACT.Silu,
                                bias=lpar("conv5_b")[:, i:i + 1])
                    ins.then_inc(ev("xbc"), 1)

                def latent_roots():
                    act.wait_ge(ev("u_part"), 8 * l + 1)
                    for t in range(NT):
                        A(area(4096 + 256 * t, 256), misc[:, t, 32:288], ACT.Square, accum_out=stats[:, 56 + t:57 + t])
                        ins = A(area(4608 + 128 * t, 128), misc[:, t, 288:416], ACT.Square, accum_out=stats[:, 58 + t:59 + t])
                    chain(ins)
                    A(stats[:, 60:62], stats[:, 56:58], ACT.Sqrt, scale=1.0 / QL, bias=eps_col)
                    A(stats[:, 62:64], stats[:, 58:60], ACT.Sqrt, scale=1.0 / KVL, bias=eps_col).then_inc(ev("lat_root"), 1)
                    act.wait_ge(ev("dt_x"), l + 1)
                    chain(A(dt_tmp, dt, ACT.Abs))
                    chain(A(dt_tmp, dt_tmp, ACT.Exp, scale=-1.0))
                    A(a_exp, lpar("a_log"), ACT.Exp)
                    A(dt_tmp, dt_tmp, ACT.Ln, bias=one_col).then_inc(ev("dt_ln"), 1)

                k4 = qk[:, 1536:3072].rearrange("p (t h d) -> p t h d", t=NT, d=AQK)

                def keys_values_of(i):
                    for t in range(NT):
                        kv = bank[KV_BANK[2 * i + t]][:, :].rearrange("p (h d) -> p h d", d=NOPE + AV)
                        A(k4[:, t, 4 * i:4 * i + 4, 0:NOPE], kv[:, :, 0:NOPE], ACT.Copy)
                        ins = A(va[:, t * 512 + i * 256:t * 512 + (i + 1) * 256].rearrange("p (h d) -> p h d", d=AV),
                                kv[:, :, NOPE:], ACT.Copy)
                    return ins

                def queries_keys(n):
                    act.wait_ge(consumed, n + 1)
                    q_rest = bank[6][:, :].rearrange("p (t n) -> p t n", t=NT)
                    for t in range(NT):
                        A(qk[:, t * 768:t * 768 + 512], bank[4 + t][:, :], ACT.Copy)
                        ins = A(qk[:, t * 768 + 512:(t + 1) * 768], q_rest[:, t, :], ACT.Copy)
                    ins.then_inc(ev("q_in"), 1)
                    keys_values_of(0).then_inc(ev("kv_in"), 1)
                    for t in range(NT):
                        A(k4[:, t, :, NOPE:], misc[:, t, 416:448].unsqueeze(1).to_broadcast([P, AH, ROPE]), ACT.Copy)

                def keys_values():
                    act.wait_ge(ev("kv_done"), l + 1)
                    keys_values_of(1).then_inc(ev("qk_in"), 1)

                def head_norms():
                    act.wait_ge(ev("qk_in"), l + 1)
                    A(qk_sq, qk, ACT.Square).then_inc(ev("qk_sq"), 1)
                    act.wait_ge(ev("qk_sum"), l + 1)
                    A(qk_root, qk_sum, ACT.Sqrt, scale=1.0 / AQK, bias=eps_col).then_inc(ev("qk_root"), 1)

                def flipped(i, dst):
                    for g in range(4):
                        act.wait_ge(ev("qk_flip"), 8 * l + 4 * i + g + 1)
                        A(dst[0:AQK, g * 512:(g + 1) * 512], bank[4 + g][0:AQK, :], ACT.Copy,
                          scale=lpar(["qh_rows", "kh_rows"][i])[0:AQK, :]).then_inc(ev("qk_t"), 1)

                def attend(t):
                    act.wait_ge(ev("peak"), 2 * l + t + 1)
                    for h in range(AH):
                        i = AH * t + h
                        ins = A(prob[:, h * S:(h + 1) * S], bank[4 + h // 2][:, (h % 2) * S:(h % 2 + 1) * S], ACT.Exp,
                                scale=q_scale[:, i:i + 1], bias=peak[:, i:i + 1], accum_out=total[:, i:i + 1])
                    ins.then_inc(ev("prob"), 1)

                def weights(t):
                    for g in range(4):
                        act.wait_ge(ev("prob_flip"), 8 * l + 4 * t + g + 1)
                        A(prob_t[:, g * 512:(g + 1) * 512], bank[4 + g][:, :], ACT.Copy).then_inc(ev("prob_t"), 1)

                def values():
                    act.wait_ge(ev("mla_y"), 2 * (l + 1))
                    A(area(0, 1024).rearrange("p (t d) -> p t d", t=NT), mix_part(D, 512, 2 * D), ACT.Square).then_inc(ev("sq"), 1)
                    root_of(1, 16, AV, l)
                    act.wait_ge(ev("conv_y"), l + 1)
                    A(area(0, 1024).rearrange("p (t d) -> p t d", t=NT), mix_part(1536, 512, 2 * D), ACT.Square).then_inc(ev("sq"), 1)
                    root_of(2, 16, 64, l)

                def rates():
                    act.wait_ge(ev("rows"), l + 1)
                    A(rows_hi, rows[0:SH, :], ACT.Copy).then_inc(ev("rows_hi"), 1)

                def tokens_x():
                    act.wait_ge(ev("xs_flip"), l + 1)
                    for t in range(NT):
                        for i in range(2):
                            ins = A(xs[:, t * D + i * 512:t * D + (i + 1) * 512], bank[4 + 2 * t + i][:, :], ACT.Copy)
                    ins.then_inc(ev("xs"), 1)
                def limit(h):
                    act.wait_ge(ev("spread"), SH * l + h + 1)
                    if h >= 3:
                        act.wait_ge(ev("y_head"), SH * l + h - 2)
                    for to, row, col, _ in spans(h):
                        ins = A(expo[h % 3][:, to], bank[4 + h % 2][:, row], ACT.Relu, scale=-1.0, bias=row_columns[:, col])
                    ins.then_inc(ev("limited"), 1)

                def head(h):
                    if h == 0:
                        limit(0)
                    act.wait_ge(ev("limited"), SH * l + h + 1)
                    e = expo[h % 3]
                    A(e, e, ACT.Exp, scale=-1.0).then_inc(ev("decays"), 1)
                    if h + 1 < SH:
                        limit(h + 1)

                steps = {
                    "latents": lambda: to_operand(8, gains_q, 3, l, KD), "head_sums": head_norms, "keys_values": keys_values,
                    **{f"silu_{c}": lambda c=c: xbc_silu(c) for c in range(1, 4)},
                    "flip_q": lambda: flipped(0, q_t), "flip_k": lambda: flipped(1, k_t),
                    "attend_0": lambda: attend(0), "weights_0": lambda: weights(0),
                    "attend_1": lambda: attend(1), "weights_1": lambda: weights(1),
                    "values": values, "rates": rates, "xs": tokens_x,
                    "early_0": lambda: head(0),
                    **{f"head_{h}": lambda h=h: head(h) for h in range(1, SH)},
                }
                for i, (c, u) in enumerate(IN_UNITS):
                    split(u0 + L_IN + i + RING)
                    if c is None:
                        queries_keys(u0 + L_IN + i)
                    elif u == 1:
                        if c not in (5, 8):
                            act.wait_ge(consumed, u0 + L_IN + i + 1)
                            tile_out(c)
                        if c == 0:
                            latent_roots()
                    for name in STEPS.get(i, []):
                        if name in steps:
                            steps[name]()
                def squares(g):
                    act.wait_ge(ev("ssd_y"), 2 * l + g + 1)
                    for t in range(NT):
                        o = mix[:, t * 2 * D + g * 512:t * 2 * D + (g + 1) * 512]
                        ins = A(va[:, t * 512:(t + 1) * 512], o, ACT.Square, accum_out=stats[:, 56 + 2 * g + t:57 + 2 * g + t])
                    chain(ins)
                    A(stats[:, 60 + 2 * g:62 + 2 * g], stats[:, 56 + 2 * g:58 + 2 * g], ACT.Sqrt, scale=1.0 / 512,
                      bias=eps_col).then_inc(ev("ssd_root"), 1)

                def take(p):
                    act.wait_ge(ev("flip"), at("flip", 11 + p, l))
                    A(xh[:, 2 * p:2 * p + 2, :], bank[MIX_BANK[p]][:, :], ACT.Copy).then_inc(ev("xh_ready"), 1)

                for h in range(HEADS_BEFORE, SH):
                    head(h)
                    if h == GATE_AFTER:
                        act.wait_ge(consumed, u0 + L_OUT)
                        tile_out(8)
                    if h == SQUARES_AFTER:
                        squares(0)
                    for p in TAKE_AFTER.get(h, []):
                        take(p)
                take(4)
                take(5)
                squares(1)
                for i in range(7):
                    split(u0 + L_OUT + i + RING)
                    if i == 0:
                        take(6)
                        take(7)
                late_norm(2, lpar("ffn2_gain"), 18, u0 + L_FFN2 + 2, l)
                if l + 1 < LAYERS:
                    act.wait_ge(ev("xl_ready"), at("xl_ready", 22, l))
                    act.dma_start(lprm[:, :], lprm_in[l + 1]).then_inc(ev("lprm_in"), 16)
                ffn(u0 + L_FFN2, (u0 + L_FFN2) // RING, FFN_BLOCKS, blk + FFN_BLOCKS, at("rstd", 2, l))

            for l in range(LAYERS):
                layer(l)

        @block.vector
        def _(dve):
            V = nc.vector
            chain = Chain(dve, "dve_chain")

            def tt(o, a, b, op):
                return V.tensor_tensor(o, a, b, op)

            def split_at(n, slot):
                dve.wait_ge(hi_done, n + 1)
                tt(lo[slot][:, :], raw[slot][:, :], hi[slot][:, :].bitcast(F32), ALU.subtract).then_inc(lo_done, 1)

            def split(n):
                if n < N_UNITS:
                    split_at(n, n % RING)

            def norm(k, gain, pairs, l=None):
                scale_rows(k, l)
                to_operand(pairs, gain, KD, l)

            def late_norm(k, gain, pairs, unit, l=None):
                to_operand(pairs, gain, KD, l)
                split(unit)
                dve.wait_ge(ev("norm_root"), at("norm_root", k + 1, l))
                V.reciprocal(rstd, root).then_inc(ev("rstd"), 1)

            def scale_rows(k, l=None):
                dve.wait_ge(ev("norm_root"), at("norm_root", k + 1, l))
                chain(V.reciprocal(rstd, root))
                for t in range(NT):
                    ins = V.tensor_scalar(mix[:, t * D:(t + 1) * D], x[:, t, :], rstd[:, t:t + 1], None, ALU.mult)
                ins.then_inc(ev("normed"), 1)

            def to_operand(pairs, gain, count, l=None, first=0, begin=0):
                for j in range(begin, count):
                    if j % 2 == 0:
                        dve.wait_ge(ev("xh_ready"), at("xh_ready", pairs + j // 2 + 1, l))
                    src = bank[4 + (j // 2) % 4]
                    if gain is None:
                        if j % 2 == 0:
                            tt(xl[:, j:j + 2, :], src[:, :].rearrange("p (j t) -> p j t", t=S),
                               xh[:, j:j + 2, :].bitcast(F32), ALU.subtract).then_inc(ev("xl_ready"), 1)
                        continue
                    ins = V.scalar_tensor_tensor(xl[:, first + j, :], src[:, (j % 2) * S:(j % 2 + 1) * S], gain[:, j:j + 1],
                                                 xh[:, first + j, :].bitcast(F32), ALU.mult, ALU.subtract)
                    if j % 2 or j == count - 1:
                        ins.then_inc(ev("xl_ready"), 1)

            def rms(values, squares, heads, width, tag, l=None):
                dve.wait_ge(ev("sq"), at("sq", tag, l))
                V.tensor_reduce(stats[:, 16:16 + heads], squares, AX.X, ALU.add).then_inc(ev("sq_sum"), 1)
                dve.wait_ge(ev("root"), at("root", tag, l))
                chain(V.reciprocal(values, stats[:, 32:32 + heads]))

            def ffn(base, nb, blk0, gated):
                def hidden(b):
                    dve.wait_ge(ev("silu"), b + blk0 + 1)
                    for t in range(NT):
                        up = bank[4 + t][:, BLK:2 * BLK]
                        if gated:
                            gate = gates[:, t, :, :].rearrange("p e b -> p (e b)")[:, bass.ds(b, 1)]
                            ins = V.scalar_tensor_tensor(hid[:, t, :], sil[:, t, :], gate, up, ALU.mult, ALU.mult)
                        else:
                            ins = V.scalar_tensor_tensor(hid[:, t, :], up, rstd[:, t:t + 1], sil[:, t, :], ALU.mult, ALU.mult)
                    ins.then_inc(ev("hid_ready"), 1)

                def rest(b):
                    dve.wait_ge(ev("hth_ready"), b + blk0 + 1)
                    tt(htl[:, :, :], bank[6][:, :].rearrange("p (f t) -> p f t", t=S),
                       hth[:, :, :].bitcast(F32), ALU.subtract).then_inc(ev("htl_ready"), 1)

                split_at(base + 3, 0)
                hidden(0)
                split_at(base + 4, 1)
                rest(0)

                def body(b):
                    split_at(b * 3 + base + 2, 2)
                    hidden(b)
                    split_at(b * 3 + base + 3, 0)
                    split_at(b * 3 + base + 4, 1)
                    rest(b)
                body(1)
                with dve.Fori(2, nb - 1) as b:
                    body(b)
                split(base + 3 * nb - 1)
                hidden(nb - 1)
                rest(nb - 1)
                split(base + 3 * nb)

            def residual(c, scale, done, count):
                dve.wait_ge(done, count)
                for t in range(NT):
                    part = x[:, t, c * 512:(c + 1) * 512]
                    ins = V.scalar_tensor_tensor(part, bank[2 * t + c][:, :], scale, part, ALU.mult, ALU.add)
                ins.then_inc(ev("x_ready" if c else "x_half"), 1)

            V.memset(eps_col, EPS)
            V.memset(one_col, 1.0)
            V.memset(restart, 1.0)
            chain(V.memset(score, 0.0))
            chain(V.memset(restart.rearrange("p (n t) -> p n t", t=P)[:, :, 0:1], 0.0))
            V.memset(stats[:, 2:3], 0.0).then_inc(ev("consts"), 1)
            scale_rows(0)
            dve.wait_ge(ev("array"), 1)
            tt(pick[:, :], ident[:, 0:SH], ident[:, 32:32 + SH], ALU.add).then_inc(ev("pick"), 1)
            dve.wait_ge(ev("params_in"), 16)
            dve.wait_ge(ev("small_hi"), 1)
            tt(small_lo[:, 0:SMALL], par("small_w"), small_hi[:, 0:SMALL].bitcast(F32), ALU.subtract).then_inc(ev("small_lo"), 1)
            lbl = par("lb_logits")
            tt(stats[:, 4:8], lbl[:, 0:HH], lbl[:, HH:2 * HH], ALU.subtract).then_inc(ev("lb_diff"), 1)
            split(0)
            to_operand(0, par("attn_gain"), KD)
            split(1)
            split(2)

            def angles():
                dve.wait_ge(ev("pos_in"), 16)
                chain(V.tensor_copy(route[:, 0:NT], pos[:, :]))
                half = ROPE // 2
                ang, turns = route[:, 16:16 + NT * half], route[:, 64:64 + NT * half]
                for t in range(NT):
                    ins = V.tensor_scalar(ang[:, t * half:(t + 1) * half], par("inv_freq"), route[:, t:t + 1], None, ALU.mult)
                chain(ins)
                for i, (quarter, shift) in enumerate([(0.25, np.pi / 2), (0.0, 0.0)]):
                    dst = trig[:, i * NT * half:(i + 1) * NT * half]
                    chain(V.tensor_scalar(turns, ang, 1 / TURN, quarter, ALU.mult, ALU.add))
                    chain(V.tensor_scalar(turns, turns, ROUND, ROUND, ALU.add, ALU.subtract))
                    chain(V.scalar_tensor_tensor(dst, turns, -TURN_HI, ang, ALU.mult, ALU.add))
                    chain(V.scalar_tensor_tensor(dst, turns, -TURN_LO, dst, ALU.mult, ALU.add))
                    chain(V.tensor_scalar(dst, dst, float(shift), PI_BELOW, ALU.add, ALU.min))
                    ins = V.tensor_scalar(dst, dst, -PI_BELOW, None, ALU.max)
                    if i == 0:
                        chain(ins)
                ins.then_inc(ev("trig_arg"), 1)

            def forget_gates():
                dve.wait_ge(ev("lb"), 1)
                chain(V.tensor_scalar(stats[:, 52:56], stats[:, 48:52], -1.0, 1.0, ALU.mult, ALU.add))
                dve.wait_ge(ev("u_out"), 1)
                for h in range(HH):
                    part = slice(h * S, (h + 1) * S)
                    ins = V.tensor_scalar(decay[1][:, part], decay[0][:, part], stats[:, 52 + h:53 + h],
                                          stats[:, 48 + h:49 + h], ALU.mult, ALU.add)
                ins.then_inc(ev("f_ready"), 1)
                dve.wait_ge(ev("fox_f"), 1)
                chain(V.tensor_scalar(route[0:FH, 0:256], bank[6][0:FH, 0:S], par("fox_bias")[0:FH, :], None, ALU.add))
                V.tensor_scalar(flog[0:FH, :], route[0:FH, 0:256], 0.0, None, ALU.min).then_inc(ev("fox_x"), 1)
                dve.wait_ge(ev("f_ready"), 1)
                chain(V.tensor_scalar(hk, decay[1], -1.0, 1.0, ALU.mult, ALU.add))

            def summed_gates():
                dve.wait_ge(ev("log_f"), 1)
                V.tensor_tensor_scan(hb, restart, decay[0], 0.0, ALU.mult, ALU.add)
                dve.wait_ge(ev("fox_ln"), 1)
                V.memset(fcum, 0.0)
                chain(tt(flog[0:FH, :], route[0:FH, 256:512], flog[0:FH, :], ALU.subtract))
                V.tensor_tensor_scan(fcum[0:FH, :], one_col[0:FH, :].to_broadcast([FH, S]), flog[0:FH, :], 0.0,
                                     ALU.mult, ALU.add).then_inc(ev("fox_cum"), 1)

            def halves(a, i):
                v = a.rearrange("p (n s t) -> p n s t", s=2, t=1 << (i - 1))
                return v[:, :, 0, :], v[:, :, 1, :]

            def diff(i):
                if i > 2:
                    dve.wait_ge(ev("level"), i - 1)
                w = 1 << (i - 1)
                n = 1024 // (2 * w)
                bl, br = halves(hb, i)
                dl, dr = halves(decay[i % 2], i)
                last = bl[:, :, w - 1:w].to_broadcast([P, n, w])
                tt(dl, last, bl, ALU.subtract)
                if i <= LEVELS:
                    ins = tt(dr, br, last, ALU.subtract)
                else:
                    ins = V.tensor_copy(dr, br)
                ins.then_inc(ev("diff"), 1)

            def weigh(i):
                dve.wait_ge(ev("decay"), i)
                dl, dr = halves(decay[i % 2], i)
                tt(dl, dl, halves(hk, i)[0], ALU.mult)
                tt(dr, dr, halves(hq, i)[1], ALU.mult).then_inc(ev("weighed"), 1)

            def keep(i):
                dve.wait_ge(ev("level"), i + 1)
                for g in range(2 if i <= LEVELS else 1):
                    src = bank[2 * (i % 2) + g][:, :]
                    if i > LEVELS:
                        ins = V.tensor_copy(cross, src)
                        continue
                    mask = level_mask[:, i * P:(i + 1) * P].bitcast(U32).unsqueeze(1).to_broadcast([P, 4, P])
                    ins = V.copy_predicated(score[:, g * 512:(g + 1) * 512].rearrange("p (n t) -> p n t", t=P),
                                            mask, src.rearrange("p (n t) -> p n t", t=P))
                ins.then_inc(ev("kept"), 1)
                dve.wait_ge(ev("kept"), i + 1)

            dve.wait_ge(ev("mask_in"), 16)
            for m in range(14):
                split(m + RING)
                if m == 0:
                    angles()
                if m == 2:
                    forget_gates()
                if m == 3:
                    summed_gates()
                if m == 4:
                    diff(1)
                    dve.wait_ge(ev("fox_cum_hi"), 1)
                    tt(fcum_lo, fcum[0:32, :], fcum_hi.bitcast(F32), ALU.subtract).then_inc(ev("fox_cum_lo"), 1)
                if m >= 6:
                    i = m - 5
                    if i <= LEVELS:
                        diff(i + 1)
                    weigh(i)
                    keep(i - 1)
            keep(LEVELS + 1)
            causal = par("causal")
            for t in range(NT):
                dve.wait_ge(ev("fox_logits"), t + 1)
                w = P * (t + 1)
                per = 512 // w
                for g in range(2 * (t + 1)):
                    ins = tt(logit[t][:, g * 512:(g + 1) * 512].rearrange("p (h s) -> p h s", s=w),
                             bank[2 * t + g][:, :].rearrange("p (h s) -> p h s", s=w),
                             causal[:, P - t * P:S].unsqueeze(1).to_broadcast([P, per, w]), ALU.add)
                chain(ins)
                top = route[:, 64 + 8 * t:72 + 8 * t]
                chain(V.tensor_reduce(top, logit[t].rearrange("p (h s) -> p h s", s=w), AX.X, ALU.max))
                V.tensor_scalar(top, top, -1.0, None, ALU.mult).then_inc(ev("fox_peak"), 1)
            rms(stats[:, 56:64], hv.rearrange("p (n d) -> p n d", d=HDK), NT * HH, HDK, 1)
            for t in range(NT):
                o3 = mix[:, t * D:t * D + 512].rearrange("p (n d) -> p n d", d=HDK)
                ins = tt(o3, bank[6 + t][:, :].rearrange("p (n d) -> p n d", d=HDK),
                         stats[:, 56 + 4 * t:60 + 4 * t].unsqueeze(2).to_broadcast([P, HH, HDK]), ALU.mult)
            ins.then_inc(ev("hg_y"), 1)
            dve.wait_ge(ev("hg_y"), 1)
            for t in range(NT):
                o3 = mix[:, t * D:t * D + 512].rearrange("p (n d) -> p n d", d=HDK)
                ins = tt(o3, o3, par("hg_gain").unsqueeze(1).to_broadcast([P, HH, HDK]), ALU.mult)
            chain(ins)
            for t in range(NT):
                ins = tt(mix[:, t * D:t * D + 512], mix[:, t * D:t * D + 512], hg[:, t * 512:(t + 1) * 512], ALU.mult)
            ins.then_inc(ev("hg_ready"), 1)
            dve.wait_ge(ev("fox_exp"), 2)
            chain(V.reciprocal(route[:, 96:112], route[:, 80:96]))
            to_operand(4, None, 4)
            dve.wait_ge(ev("fox_o"), 1)
            for t in range(NT):
                ins = tt(mix[:, t * D + 512:(t + 1) * D].rearrange("p (h d) -> p h d", d=FDH),
                         bank[6 + t][:, :].rearrange("p (h d) -> p h d", d=FDH),
                         route[:, 96 + 8 * t:104 + 8 * t].unsqueeze(2).to_broadcast([P, FH, FDH]), ALU.mult)
            ins.then_inc(ev("fox_norm"), 1)
            dve.wait_ge(ev("fox_norm"), 1)
            rms(route[:, 112:128], logit[0].rearrange("p (n d) -> p n d", d=FDH), NT * FH, FDH, 2)
            for t in range(NT):
                o3 = mix[:, t * D + 512:(t + 1) * D].rearrange("p (h d) -> p h d", d=FDH)
                chain(tt(o3, o3, route[:, 112 + 8 * t:120 + 8 * t].unsqueeze(2).to_broadcast([P, FH, FDH]), ALU.mult))
                ins = tt(o3, o3, par("fox_gain").unsqueeze(1).to_broadcast([P, FH, FDH]), ALU.mult)
            ins.then_inc(ev("mixed"), 1)
            to_operand(4, None, KD, begin=4)
            for i in range(4):
                if i % 2:
                    residual(i // 2, 1.0, consumed, U_OUT1 + i + 1)
                if i < 3:
                    split(U_OUT1 + i + RING)
            late_norm(1, par("ffn_gain"), 8, U_MOE + 2)
            dve.wait_ge(ev("rstd"), 1)

            dve.wait_ge(ev("route_rows"), 1)
            V.tensor_copy(area(D, S)[0:NG + NE, :], bank[6][0:NG + NE, 0:S]).then_inc(ev("route_copy"), 1)
            dve.wait_ge(ev("routed"), 1)
            r3 = lambda a, n: route[:, a:a + NT * n].rearrange("p (t n) -> p t n", n=n)
            lg = r3(0, NG + NE)
            for t in range(NT):
                ins = V.scalar_tensor_tensor(lg[:, t, :], bank[7][:, t * (NG + NE):(t + 1) * (NG + NE)], rstd[:, t:t + 1],
                                             par("router_bias"), ALU.mult, ALU.add)
            chain(ins)
            lgg = lg[:, :, 0:NG]
            desc = par("desc4").unsqueeze(1).to_broadcast([P, NT, 4])

            def best(values, peak, onehot, tmp):
                chain(V.tensor_reduce(peak, values, AX.X, ALU.max))
                chain(tt(tmp, values, peak.unsqueeze(2).to_broadcast([P, NT, 4]), ALU.is_equal))
                chain(tt(tmp, tmp, desc, ALU.mult))
                chain(V.tensor_reduce(route[:, 136:138], tmp, AX.X, ALU.max))
                chain(tt(onehot, tmp, route[:, 136:138].unsqueeze(2).to_broadcast([P, NT, 4]), ALU.is_equal))

            r4 = lambda a: route[:, a:a + 8].rearrange("p (t n) -> p t n", n=4)
            best(lgg, route[:, 56:58], r4(60), r4(68))
            tt(r4(40), lgg, route[:, 56:58].unsqueeze(2).to_broadcast([P, NT, 4]), ALU.subtract).then_inc(ev("route_g"), 1)
            picked = route[:, 144:176].rearrange("p (t e g) -> p t e g", t=NT, e=4)
            for t in range(NT):
                ins = tt(picked[:, t, :, :], lg[:, t, NG:NG + NE].rearrange("p (g e) -> p e g", e=4),
                         r4(60)[:, t, :].unsqueeze(1).to_broadcast([P, 4, 4]), ALU.mult)
            chain(ins)
            chain(V.tensor_reduce(route[:, 76:84], route[:, 144:176].rearrange("p (n g) -> p n g", g=4), AX.X, ALU.add))
            best(r4(76), route[:, 84:86], r4(88), r4(68))
            chain(V.scalar_tensor_tensor(route[:, 96:104], route[:, 88:96], -BIG, route[:, 76:84], ALU.mult, ALU.add))
            best(r4(96), route[:, 86:88], r4(104), r4(68))
            tt(route[:, 118:120], route[:, 86:88], route[:, 84:86], ALU.subtract).then_inc(ev("route_e"), 1)
            dve.wait_ge(ev("route_ge"), 1)
            chain(V.tensor_reduce(route[:, 112:114], r4(48), AX.X, ALU.add))
            dve.wait_ge(ev("route_ee"), 1)
            chain(V.tensor_scalar(route[:, 122:124], route[:, 120:122], 1.0, None, ALU.add))
            chain(tt(route[:, 122:124], route[:, 122:124], route[:, 112:114], ALU.mult))
            chain(V.reciprocal(route[:, 124:126], route[:, 122:124]))
            chain(tt(route[:, 126:128], route[:, 124:126], route[:, 120:122], ALU.mult))
            chain(tt(r4(88), r4(88), route[:, 124:126].unsqueeze(2).to_broadcast([P, NT, 4]), ALU.mult))
            chain(tt(r4(104), r4(104), route[:, 126:128].unsqueeze(2).to_broadcast([P, NT, 4]), ALU.mult))
            chain(tt(r4(88), r4(88), r4(104), ALU.add))
            chain(tt(r4(88), r4(88), rstd.unsqueeze(2).to_broadcast([P, NT, 4]), ALU.mult))
            for t in range(NT):
                for g in range(NG):
                    for e in range(2):
                        ins = tt(gates[:, t, 4 * g:4 * g + 4, e], r4(88)[:, t, :],
                                 r4(60)[:, t, g:g + 1].to_broadcast([P, 4]), ALU.mult)
            chain(ins)
            ffn(U_MOE, MOE_BLOCKS, 0, True)
            residual(0, 1.0, ev("y_half"), 1)
            residual(1, 1.0, consumed, U_LAYER)
            dve.wait_ge(ev("final_in"), 16)
            dve.wait_ge(ev("norm_root"), 3)
            chain(V.reciprocal(rstd, root))
            for t in range(NT):
                ins = V.scalar_tensor_tensor(x[:, t, :], x[:, t, :], rstd[:, t:t + 1], final_gain, ALU.mult, ALU.mult)
            ins.then_inc(ev("x_ready"), 1)

            def layer(l):
                u0 = U_LAYER + L_UNITS * l
                blk = MOE_BLOCKS + 2 * FFN_BLOCKS * l
                dve.wait_ge(ev("lprm_in"), 16 * (l + 1))
                late_norm(0, lpar("ffn1_gain"), 0, u0 + 1, l)
                split(u0 + 2)
                ffn(u0, FFN_BLOCKS, blk, False)
                residual(0, 0.5, ev("y_half"), at("y_half", 1, l))
                residual(1, 0.5, consumed, u0 + L_IN)
                dve.wait_ge(ev("ukv_hi"), l + 1)
                tt(small_lo[:, :], ukv_raw, small_hi[:, :].bitcast(F32), ALU.subtract).then_inc(ev("ukv_lo"), 1)
                split(u0 + L_IN + 1)
                norm(1, lpar("mix_gain"), 4, l)
                split(u0 + L_IN + 2)
                m3 = lambda a: a.rearrange("p (t n) -> p t n", t=NT)

                def taps(src, dst, w, first, count, signal):
                    mid = count // 2
                    order = [k for k in range(count) if k != mid]
                    for j, k in enumerate(order if count == 5 else [mid] + order, count == 5):
                        for i in range(4):
                            wk = w[:, (first + i) * count + k:(first + i) * count + k + 1]
                            t0, t1 = max(0, mid - k), S - max(0, k - mid)
                            o = dst[:, i * S + t0:i * S + t1]
                            a = src[:, i * S + t0 + k - mid:i * S + t1 + k - mid]
                            if j == 0:
                                ins = V.tensor_scalar(o, a, wk, None, ALU.mult)
                            else:
                                ins = V.scalar_tensor_tensor(o, a, wk, o, ALU.mult, ALU.add)
                        if j == count - 1:
                            ins.then_inc(signal, 1)
                        else:
                            chain(ins)

                def xbc_taps(c):
                    dve.wait_ge(ev("u_part"), 8 * l + c + 1)
                    taps(conv_buf[(c + 1) % 2], xbc[:, (c - 1) * D:c * D], lpar("conv5_w"), 4 * c - 4, 5, ev("conv5"))

                def latents():
                    dve.wait_ge(ev("u_part"), 8 * l + 1)
                    chain(tt(m3(dt), misc[:, :, 0:32], lpar("dt_bias").unsqueeze(1).to_broadcast([P, NT, 32]), ALU.add))
                    V.tensor_scalar(dt_a, dt, 0.0, None, ALU.max).then_inc(ev("dt_x"), 1)
                    dve.wait_ge(ev("lat_root"), l + 1)
                    chain(V.reciprocal(stats[:, 56:60], stats[:, 60:64]))
                    for t in range(NT):
                        V.tensor_scalar(misc[:, t, 32:288], misc[:, t, 32:288], stats[:, 56 + t:57 + t], None, ALU.mult)
                        ins = V.tensor_scalar(misc[:, t, 288:416], misc[:, t, 288:416], stats[:, 58 + t:59 + t], None, ALU.mult)
                    ins.then_inc(ev("lat"), 1)

                def head_norms():
                    dve.wait_ge(ev("qk_sq"), l + 1)
                    V.tensor_reduce(qk_sum, qk_sq.rearrange("p (n d) -> p n d", d=AQK), AX.X, ALU.add).then_inc(ev("qk_sum"), 1)
                    dve.wait_ge(ev("qk_root"), l + 1)
                    chain(V.reciprocal(qk_rstd, qk_root))
                    V.tensor_scalar(q_scale, qk_rstd[:, 0:16], AQK ** -0.5, None, ALU.mult)
                    k3 = qk[:, 1536:3072].rearrange("p (n d) -> p n d", d=AQK)
                    chain(tt(k3, k3, qk_rstd[:, 16:32].unsqueeze(2).to_broadcast([P, 2 * AH, AQK]), ALU.mult))

                def gained_turns():
                    half = ROPE // 2
                    dve.wait_ge(ev("trig"), 1)
                    for dst, (part, second) in zip(turns_by, [(0, 0), (1, 1), (1, 0), (0, 1)]):
                        for i, name in enumerate(["qh_rope", "kh_rope"]):
                            ins = tt(dst[:, i, :, :], trig[:, part * NT * half:(part + 1) * NT * half].rearrange("p (t d) -> p t d", t=NT),
                                     lpar(name)[:, second * half:(second + 1) * half].unsqueeze(1).to_broadcast([P, NT, half]), ALU.mult)
                    chain(ins)

                def rotate():
                    half = ROPE // 2
                    q5 = qk.rearrange("p (i t h d) -> p i t h d", i=2, t=NT, d=AQK)
                    for t in range(NT):
                        lo_, hi_ = q5[:, :, t, :, NOPE:NOPE + half], q5[:, :, t, :, NOPE + half:AQK]
                        tmp = [area(3072 + 256 * (4 * t + i), 256).rearrange("p (i h d) -> p i h d", i=2, d=half)
                               for i in range(4)]
                        for i, src in enumerate([lo_, hi_, lo_, hi_]):
                            ins = tt(tmp[i], src, turns_by[i][:, :, t, :].unsqueeze(2).to_broadcast([P, 2, AH, half]), ALU.mult)
                        chain(ins)
                        tt(lo_, tmp[0], tmp[1], ALU.subtract)
                        ins = tt(hi_, tmp[2], tmp[3], ALU.add)
                    ins.then_inc(ev("qk"), 1)

                def attend(t):
                    dve.wait_ge(ev("logits"), 2 * l + t + 1)
                    for g in range(4):
                        ins = V.tensor_reduce(peak[:, 8 * t + 2 * g:8 * t + 2 * g + 2],
                                              bank[4 + g][:, :].rearrange("p (h s) -> p h s", s=S), AX.X, ALU.max)
                    chain(ins)
                    part = slice(8 * t, 8 * t + 8)
                    V.scalar_tensor_tensor(peak[:, part], peak[:, part], -1.0, q_scale[:, part], ALU.mult,
                                           ALU.mult).then_inc(ev("peak"), 1)

                def a3(t):
                    return mix[:, t * 2 * D + D:t * 2 * D + D + 512].rearrange("p (h d) -> p h d", d=AV)

                def weigh(t):
                    dve.wait_ge(ev("prob"), 2 * l + t + 1)
                    chain(V.reciprocal(ob_rstd[:, 0:8], total[:, 8 * t:8 * t + 8]))
                    dve.wait_ge(ev("mla_o"), 2 * l + t + 1)
                    tt(a3(t), bank[4][:, :].rearrange("p (h d) -> p h d", d=AV),
                       ob_rstd[:, 0:8].unsqueeze(2).to_broadcast([P, AH, AV]), ALU.mult).then_inc(ev("mla_y"), 1)

                def values():
                    dve.wait_ge(ev("mla_y"), 2 * (l + 1))
                    rms(ob_rstd, area(0, 1024).rearrange("p (n d) -> p n d", d=AV), 16, AV, 1, l)
                    for t in range(NT):
                        ins = tt(a3(t), a3(t), ob_rstd[:, 8 * t:8 * t + 8].unsqueeze(2).to_broadcast([P, AH, AV]), ALU.mult)
                    chain(ins)
                    m5 = mix_part(D, 512, 2 * D)
                    tt(m5, m5, lpar("mla_gain").unsqueeze(1).to_broadcast([P, NT, 512]), ALU.mult)
                    dve.wait_ge(ev("c_flip"), l + 1)
                    dve.wait_ge(ev("u_part"), 8 * l + 6)
                    for t in range(NT):
                        part = mix[:, t * 2 * D + 1536:(t + 1) * 2 * D]
                        ins = tt(part, part, bank[6 + t][:, :], ALU.mult)
                    ins.then_inc(ev("conv_y"), 1)
                    dve.wait_ge(ev("conv_y"), l + 1)
                    rms(ob_rstd, area(0, 1024).rearrange("p (n d) -> p n d", d=64), 16, 64, 2, l)
                    for t in range(NT):
                        g3 = mix[:, t * 2 * D + 1536:(t + 1) * 2 * D].rearrange("p (n d) -> p n d", d=64)
                        ins = tt(g3, g3, ob_rstd[:, 8 * t:8 * t + 8].unsqueeze(2).to_broadcast([P, 8, 64]), ALU.mult)
                    chain(ins)
                    c5 = mix_part(1536, 512, 2 * D)
                    tt(c5, c5, lpar("conv_gain").unsqueeze(1).to_broadcast([P, NT, 512]), ALU.mult).then_inc(ev("side"), 1)

                def rates():
                    dve.wait_ge(ev("dt_flip"), l + 1)
                    f, b = slice(0, S), slice(S, 2 * S)
                    chain(V.tensor_copy(rate[0:SH, :], bank[5][0:SH, :]))
                    for part in (f, b):
                        ins = V.tensor_tensor_scan(cum[0:SH, part], one_col[0:SH, :].to_broadcast([SH, S]), rate[0:SH, part],
                                                   0.0, ALU.mult, ALU.add)
                    chain(ins)
                    V.tensor_copy(rows[0:SH, f], cum[0:SH, f])
                    tt(rows[0:SH, b], rate[0:SH, b], cum[0:SH, b], ALU.subtract).then_inc(ev("rows"), 1)
                    dve.wait_ge(ev("rows_flip"), l + 1)
                    V.tensor_copy(row_columns, bank[4][:, 0:64]).then_inc(ev("row_cols"), 1)
                    dve.wait_ge(ev("rows_hi"), l + 1)
                    tt(rows_lo, rows[0:SH, :], rows_hi.bitcast(F32), ALU.subtract).then_inc(ev("rows_lo"), 1)

                def heads(a):
                    return a.rearrange("p (h d) -> p h d", d=SP_)

                def masked_cb():
                    dve.wait_ge(ev("cb"), l + 1)
                    for g in range(SG):
                        cb, src = cb_score[:, g * 768:(g + 1) * 768], bank[6 + g]
                        tt(cb[:, 0:128], src[:, 0:128], future, ALU.mult)
                        V.tensor_copy(cb[:, 128:384], src[:, 128:384])
                        tt(cb[:, 384:512], src[:, 384:512], past, ALU.mult)
                        tt(cb[:, 512:640], src[:, 0:128], past, ALU.mult)
                        ins = tt(cb[:, 640:768], src[:, 384:512], future, ALU.mult)
                    ins.then_inc(ev("cb_out"), 1)
                    for t in range(NT):
                        ins = tt(heads(skip[:, t * D:(t + 1) * D]), heads(xs[:, t * D:(t + 1) * D]),
                                 lpar("d_skip").unsqueeze(2).to_broadcast([P, SH, SP_]), ALU.mult)
                    chain(ins)
                    dve.wait_ge(ev("cb_out"), l + 1)

                def head(h):
                    e, g = expo[h % 3], h // 8
                    dve.wait_ge(ev("decays"), SH * l + h + 1)
                    for to, _, _, col in spans(h):
                        ins = V.scalar_tensor_tensor(e[:, to], e[:, to], dt[:, col], cb_score[:, g * 768 + to.start:g * 768 + to.stop],
                                                     ALU.mult, ALU.mult)
                    chain(ins)
                    within = e.rearrange("p (t n) -> p t n", t=NT)[:, :, 0:P]
                    tt(within, within, e[:, 512:768].rearrange("p (t n) -> p t n", t=NT), ALU.add).then_inc(ev("scores"), 1)
                    if h % 8 == 7:
                        dve.wait_ge(ev("y_head"), SH * l + h + 1)
                        for t in range(NT):
                            o = mix[:, t * 2 * D + g * 512:t * 2 * D + (g + 1) * 512]
                            ins = tt(o, bank[6 + t][:, :], skip[:, t * D + g * 512:t * D + (g + 1) * 512], ALU.add)
                        ins.then_inc(ev("y_out"), 1)

                steps = {
                    "latents": lambda: to_operand(8, gains_q, 3, l, KD), "head_sums": head_norms, "rotate": rotate,
                    **{f"taps_{c}": lambda c=c: xbc_taps(c) for c in range(1, 4)},
                    "attend_0": lambda: attend(0), "attend_1": lambda: attend(1),
                    "weigh_0": lambda: weigh(0), "weigh_1": lambda: weigh(1),
                    "values": values, "rates": rates, "cb": masked_cb,
                    "early_0": lambda: head(0),
                    **{f"head_{h}": lambda h=h: head(h) for h in range(1, SH)},
                }
                for i, (c, u) in enumerate(IN_UNITS):
                    split(u0 + L_IN + i + RING)
                    if u == 1 and c == 0:
                        latents()
                        dve.wait_ge(ev("dt_ln"), l + 1)
                        gained_turns()
                        chain(tt(dt, dt_a, dt_tmp, ALU.add))
                        V.scalar_tensor_tensor(m3(dt_a), m3(dt), -1.0, a_exp.unsqueeze(1).to_broadcast([P, NT, 32]),
                                               ALU.mult, ALU.mult).then_inc(ev("dt_a"), 1)
                    if u == 1 and c == 5:
                        dve.wait_ge(ev("u_part"), 8 * l + 5)
                        dve.wait_ge(consumed, u0 + L_IN + i + 1)
                        for j in range(2):
                            part = conv_buf[1][:, j * 512:(j + 1) * 512]
                            ins = tt(part, part, bank[2 + j][:, :], ALU.mult)
                        ins.then_inc(ev("c_prod"), 1)
                        dve.wait_ge(ev("c_prod"), l + 1)
                        taps(conv_buf[1], conv_buf[0], lpar("conv3_w"), 0, 3, ev("conv3"))
                    for name in STEPS.get(i, []):
                        if name in steps:
                            steps[name]()
                def gated(g):
                    dve.wait_ge(ev("y_out"), 2 * l + g + 1)
                    dve.wait_ge(ev("u_part"), 8 * l + 7 + g)
                    for t in range(NT):
                        o = mix[:, t * 2 * D + g * 512:t * 2 * D + (g + 1) * 512]
                        ins = tt(o, o, zs[:, t * D + g * 512:t * D + (g + 1) * 512], ALU.mult)
                    ins.then_inc(ev("ssd_y"), 1)

                def normed_group(g):
                    dve.wait_ge(ev("ssd_root"), 2 * l + g + 1)
                    chain(V.reciprocal(ob_rstd[:, 2 * g:2 * g + 2], stats[:, 60 + 2 * g:62 + 2 * g]))
                    for t in range(NT):
                        o = mix[:, t * 2 * D + g * 512:t * 2 * D + (g + 1) * 512]
                        ins = V.scalar_tensor_tensor(o, o, ob_rstd[:, 2 * g + t:2 * g + t + 1],
                                                     lpar("ssd_gain")[:, g * 512:(g + 1) * 512], ALU.mult, ALU.mult)
                    ins.then_inc(ev("group"), 1)

                def take(p):
                    dve.wait_ge(ev("xh_ready"), at("xh_ready", 11 + p, l))
                    tt(xl[:, 2 * p:2 * p + 2, :], bank[MIX_BANK[p]][:, :].rearrange("p (j t) -> p j t", t=S),
                       xh[:, 2 * p:2 * p + 2, :].bitcast(F32), ALU.subtract).then_inc(ev("xl_ready"), 1)

                for h in range(HEADS_BEFORE, SH):
                    head(h)
                    if h == 8:
                        gated(0)
                    for p in TAKE_AFTER.get(h, []):
                        take(p)
                    if h == NORM_AFTER:
                        normed_group(0)
                gated(1)
                take(4)
                take(5)
                normed_group(1)
                for i in range(8):
                    if i % 4 == 3:
                        residual(i // 4, 1.0, consumed, u0 + L_OUT + i + 1)
                    if i < 7:
                        split(u0 + L_OUT + i + RING)
                    if i == 0:
                        take(6)
                        take(7)
                late_norm(2, lpar("ffn2_gain"), 18, u0 + L_FFN2 + 2, l)
                ffn(u0 + L_FFN2, FFN_BLOCKS, blk + FFN_BLOCKS, False)
                residual(0, 0.5, ev("y_half"), at("y_half", 2, l))
                residual(1, 0.5, consumed, u0 + L_UNITS)

            for l in range(LAYERS):
                layer(l)
            dve.wait_ge(ev("x_ready"), at("x_ready", 0, LAYERS))
            V.memset(stats[:, 3:4], 0.0).then_inc(ev("result"), 1)

        @block.tensor
        def _(pe):
            mm, flip_of = nc.tensor.matmul, nc.tensor.transpose

            def three(o, a_hi, a_lo, b_hi, b_lo, start, stop_, shared=False):
                mm(o, a_lo, b_hi, start=start, stop=False, skip_group_check=shared)
                mm(o, a_hi, b_lo, start=False, stop=False, skip_group_check=shared)
                return mm(o, a_hi, b_hi, start=False, stop=stop_, skip_group_check=shared)

            def tokens(a, j, t):
                return a[:, j, t * P:(t + 1) * P]

            def unit_tm(n, u, pair, width=512):
                s = n % RING
                pe.wait_ge(lo_done, n + 1)
                for t in range(NT):
                    for j in range(4):
                        c = slice(j * 512, j * 512 + width)
                        k = 4 * u + j
                        ins = three(bank[pair + t][:, 0:width], tokens(xh, k, t), tokens(xl, k, t),
                                    hi[s][:, c], lo[s][:, c], k == 0, k == 7)
                ins.then_inc(consumed, 1)

            def unit_fm(n, u, pair, width=512):
                s = n % RING
                pe.wait_ge(lo_done, n + 1)
                for f in range(4):
                    o = bank[pair + f // 2][:, (f % 2) * S:(f % 2 + 1) * S]
                    for j in range(4):
                        c = slice(j * 512 + f * P, j * 512 + (f + 1) * P)
                        k = 4 * u + j
                        ins = three(o, hi[s][:, c], lo[s][:, c], xh[:, k, :], xl[:, k, :],
                                    k == 0 and f % 2 == 0, k == 7, True)
                ins.then_inc(consumed, 1)

            def small_rows(o, c, width):
                for k in range(KD):
                    cc = slice(k * 28 + c, k * 28 + c + width)
                    ins = three(o, small_hi[:, cc], small_lo[:, cc], xh[:, k, :], xl[:, k, :], k == 0, k == 7)
                return ins

            def to_operand(pairs, src, count, l=None, begin=0):
                for j in range(begin, count, 2):
                    if j >= 8:
                        pe.wait_ge(ev("xl_ready"), at("xl_ready", pairs + j // 2 - 3, l))
                    for jj in range(min(2, count - j)):
                        for t in range(NT):
                            ins = flip_of(bank[4 + (j // 2) % 4][:, jj * S + t * P:jj * S + (t + 1) * P], src(t, j + jj), ident)
                    ins.then_inc(ev("flip"), 1)

            def norm(k, pairs, l=None):
                pe.wait_ge(ev("normed"), at("normed", 1, l))
                to_operand(pairs, lambda t, j: mix[:, t * D + j * P:t * D + (j + 1) * P], KD, l)
                pe.wait_ge(ev("xl_ready"), at("xl_ready", pairs + 2, l))

            def late_norm(k, pairs, l=None):
                if l != 0 or k:
                    pe.wait_ge(ev("x_half"), at("x_half", k, l))
                else:
                    pe.wait_ge(ev("x_ready"), at("x_ready", k, l))

                def columns_of(t, j):
                    if j == 4 and t == 0:
                        pe.wait_ge(ev("x_ready"), at("x_ready", k, l))
                    return x[:, t, j * P:(j + 1) * P]
                to_operand(pairs, columns_of, KD, l)
                pe.wait_ge(ev("xl_ready"), at("xl_ready", pairs + 2, l))

            def out_product(n0, units_each, between=None):
                for c in range(2):
                    for u in range(units_each):
                        if between is not None:
                            between(c, u)
                        n = n0 + c * units_each + u
                        s = n % RING
                        pe.wait_ge(lo_done, n + 1)
                        for t in range(NT):
                            for j in range(4):
                                k = 4 * u + j
                                cc = slice(j * 512, (j + 1) * 512)
                                ins = three(bank[2 * t + c][:, :], tokens(xh, k, t), tokens(xl, k, t),
                                            hi[s][:, cc], lo[s][:, cc], k == 0, k == 4 * units_each - 1)
                        ins.then_inc(consumed, 1)

            def ffn(base, nb, blk0, operand):
                def gate_up(b, n, slots, first):
                    for u, s in enumerate(slots):
                        pe.wait_ge(lo_done, n + u + 1)
                        if u == 0 and not first:
                            pe.wait_ge(ev("hid_ready"), b + blk0)
                        if u == 1 and first:
                            pe.wait_ge(ev("xl_ready"), operand)
                        for t in range(NT):
                            for j in range(4):
                                k = 4 * u + j
                                c = slice(j * 512, (j + 1) * 512)
                                ins = three(bank[4 + t][:, :], tokens(xh, k, t), tokens(xl, k, t),
                                            hi[s][:, c], lo[s][:, c], k == 0, k == KD - 1)
                        ins.then_inc(consumed, 1)

                def down(b, n, s, first):
                    pe.wait_ge(lo_done, n + 1)
                    pe.wait_ge(ev("htl_ready"), b + blk0 + 1)
                    for f in range(2):
                        for t in range(NT):
                            for c in range(2):
                                ins = down_product(s, f, t, c, first and f == 0, False)
                    ins.then_inc(consumed, 1)

                def down_product(s, f, t, c, start, stop_):
                    cc = slice(f * D + c * 512, f * D + (c + 1) * 512)
                    return three(bank[2 * t + c][:, :], tokens(hth, f, t), tokens(htl, f, t),
                                 hi[s][:, cc], lo[s][:, cc], start, stop_, True)

                def last_down(b, n, s):
                    pe.wait_ge(lo_done, n + 1)
                    pe.wait_ge(ev("htl_ready"), b + blk0 + 1)
                    for c in range(2):
                        for t in range(NT):
                            for f in range(2):
                                ins = down_product(s, f, t, c, False, f == 1)
                        if c == 0:
                            ins.then_inc(ev("y_half"), 1)
                    ins.then_inc(consumed, 1)

                def hidden(b):
                    pe.wait_ge(ev("hid_ready"), b + blk0 + 1)
                    for f in range(2):
                        for t in range(NT):
                            ins = flip_of(bank[6][:, f * S + t * P:f * S + (t + 1) * P], hid[:, t, f * P:(f + 1) * P], ident)
                    ins.then_inc(ev("hid_flip"), 1)

                gate_up(0, base, [0, 1], True)
                hidden(0)

                def body(b, first=False):
                    gate_up(b, b * 3 + base - 1, [2, 0], False)
                    down(b - 1, b * 3 + base + 1, 1, first)
                    hidden(b)
                body(1, True)
                with pe.Fori(2, nb) as b:
                    body(b)
                last_down(nb - 1, base + 3 * nb - 1, 2)

            pe.wait_ge(ev("array"), 1)
            norm(0, 0)

            def level(i):
                if i == 0:
                    pe.wait_ge(ev("diff"), 1)
                    pe.wait_ge(ev("u_out"), 2)
                else:
                    pe.wait_ge(ev("weighed"), i)
                if i >= 2:
                    pe.wait_ge(ev("kept"), i - 1)
                for g in range(8):
                    c = slice(g * P, (g + 1) * P)
                    src = decay[i % 2]
                    o = bank[2 * (i % 2) + g // 4][:, (g % 4) * P:(g % 4 + 1) * P]
                    if i == 0:
                        ins = mm(o, hk[:, c], hq[:, c], start=True, stop=True)
                    elif i <= LEVELS:
                        ins = mm(o, src[:, c], src[:, c], start=True, stop=True)
                    elif g < HH:
                        ins = mm(bank[2 * (i % 2)][:, g * P:(g + 1) * P], src[:, 2 * g * P:(2 * g + 1) * P],
                                 src[:, (2 * g + 1) * P:(2 * g + 2) * P], start=True, stop=True)
                ins.then_inc(ev("level"), 1)

            for m in range(14):
                i, u = m // 2, m % 2
                if i >= 4 and u == 0:
                    pe.wait_ge(ev("u_out"), i - 1)
                if i == 3 and u == 0:
                    pe.wait_ge(ev("fox_x"), 1)
                if m == 1:
                    pe.wait_ge(ev("xl_ready"), 4)
                (unit_fm if IN1_TILES[i] in (0, 1, 4, 5) else unit_tm)(m, u, IN1_PAIR[i])
                if m == 1:
                    pe.wait_ge(ev("small_lo"), 1)
                    small_rows(bank[6][0:FH, 0:S], 0, FH).then_inc(ev("fox_f"), 1)
                if m >= 6:
                    level(m - 6)
            level(LEVELS + 1)
            pe.wait_ge(ev("kept"), LEVELS + 2)
            pe.wait_ge(ev("u_out"), 7)
            pe.wait_ge(ev("pick"), 1)
            pe.wait_ge(ev("fox_cum_lo"), 1)
            for t in range(NT):
                w = P * (t + 1)
                for h in range(FH):
                    per = 512 // w
                    o = bank[2 * t + h // per][:, (h % per) * w:(h % per + 1) * w]
                    mm(o, fq[:, h * S + t * P:h * S + (t + 1) * P], fk[:, (h // 2) * S:(h // 2) * S + w],
                       start=True, stop=False)
                    ins = mm(o, pick[0:64, h:h + 1].to_broadcast([64, P]), fcum_both[:, 0:w], start=False, stop=True)
                ins.then_inc(ev("fox_logits"), 1)
            for h in range(HH):
                c = slice(h * P, (h + 1) * P)
                v = [hv[:, t * 512 + h * P:t * 512 + (h + 1) * P] for t in range(NT)]
                mm(bank[6][:, c], score[:, 2 * h * P:(2 * h + 1) * P], v[0], start=True, stop=True)
                mm(bank[7][:, c], cross[:, c], v[0], start=True, stop=False)
                ins = mm(bank[7][:, c], score[:, (2 * h + 1) * P:(2 * h + 2) * P], v[1], start=False, stop=True)
            ins.then_inc(ev("hg_o"), 1)
            for g in range(6):
                pe.wait_ge(ev("fox_exp"), 1 if g < 2 else 2)
                for i in range(4):
                    q = 4 * g + i
                    src = logit[0][:, q * P:(q + 1) * P] if q < 8 else logit[1][:, (q - 8) * P:(q - 7) * P]
                    ins = flip_of(bank[g][:, i * P:(i + 1) * P], src, ident)
                ins.then_inc(ev("fox_flip"), 1)
            pe.wait_ge(ev("fox_pT"), 6)
            pe.wait_ge(ev("hg_ready"), 1)
            to_operand(4, lambda t, j: mix[:, t * D + j * P:t * D + (j + 1) * P], 4)
            pe.wait_ge(ev("hg_y"), 1)
            for h in range(FH):
                c = slice(h * FDH, (h + 1) * FDH)
                v = [fv[:, t * 512 + h * FDH:t * 512 + (h + 1) * FDH] for t in range(NT)]
                mm(bank[6][:, c], probT[:, h * P:(h + 1) * P], v[0], start=True, stop=True)
                mm(bank[7][:, c], probT[:, (8 + 2 * h) * P:(9 + 2 * h) * P], v[0], start=True, stop=False)
                ins = mm(bank[7][:, c], probT[:, (9 + 2 * h) * P:(10 + 2 * h) * P], v[1], start=False, stop=True)
            ins.then_inc(ev("fox_o"), 1)

            def halves_of(c, u):
                if (c, u) == (0, 0):
                    pe.wait_ge(ev("xl_ready"), 6)
                if (c, u) == (0, 1):
                    pe.wait_ge(ev("mixed"), 1)
                    to_operand(4, lambda t, j: mix[:, t * D + j * P:t * D + (j + 1) * P], KD, begin=4)
                    pe.wait_ge(ev("xl_ready"), 8)
            out_product(U_OUT1, 2, halves_of)
            late_norm(1, 8)
            pe.wait_ge(ev("xl_ready"), 12)
            small_rows(bank[6][0:NG + NE, 0:S], FH, NG + NE).then_inc(ev("route_rows"), 1)
            pe.wait_ge(ev("route_copy"), 1)
            for t in range(NT):
                ins = flip_of(bank[7][:, t * 20:(t + 1) * 20], area(D, S)[0:NG + NE, t * P:(t + 1) * P],
                              ident[0:NG + NE, 0:NG + NE])
            ins.then_inc(ev("routed"), 1)
            ffn(U_MOE, MOE_BLOCKS, 0, 12)

            def layer(l):
                u0 = U_LAYER + L_UNITS * l
                blk = MOE_BLOCKS + 2 * FFN_BLOCKS * l
                late_norm(0, 0, l)
                ffn(u0, FFN_BLOCKS, blk, at("xl_ready", 4, l))
                norm(1, 4, l)

                def latents():
                    pe.wait_ge(ev("lat"), l + 1)
                    to_operand(8, lambda t, j: misc[:, t, 32 + j * P:32 + (j + 1) * P], 3, l)

                def mla_products(n):
                    s = n % RING
                    pe.wait_ge(ev("xl_ready"), at("xl_ready", 10, l))
                    pe.wait_ge(lo_done, n + 1)
                    for t in range(NT):
                        for k in range(2):
                            c = slice(k * 768, k * 768 + 512)
                            three(bank[4 + t][:, :], tokens(xh, KD + k, t), tokens(xl, KD + k, t), hi[s][:, c], lo[s][:, c], k == 0, k == 1)
                    for t in range(NT):
                        for k in range(2):
                            c = slice(k * 768 + 512, (k + 1) * 768)
                            three(bank[6][:, t * 256:(t + 1) * 256], tokens(xh, KD + k, t), tokens(xl, KD + k, t),
                                  hi[s][:, c], lo[s][:, c], k == 0, k == 1)
                    pe.wait_ge(ev("u_part"), 8 * l + 2)
                    for t in range(NT):
                        ins = three(bank[KV_BANK[t]][:, :], tokens(xh, KD + 2, t), tokens(xl, KD + 2, t),
                                    hi[s][:, 1536:], lo[s][:, 1536:], True, True)
                    ins.then_inc(consumed, 1)

                def keys_values():
                    pe.wait_ge(ev("q_in"), l + 1)
                    pe.wait_ge(ev("ukv_lo"), l + 1)
                    for t in range(NT):
                        ins = three(bank[KV_BANK[2 + t]][:, :], tokens(xh, KD + 2, t), tokens(xl, KD + 2, t),
                                    small_hi[:, :], small_lo[:, :], True, True)
                    ins.then_inc(ev("kv_done"), 1)

                def flip_heads(i):
                    if i == 0:
                        pe.wait_ge(ev("qk"), l + 1)
                    else:
                        pe.wait_ge(ev("qk_t"), 8 * l + 4)
                    for g in range(4):
                        for h in range(2):
                            for t in range(NT):
                                a = i * 1536 + t * 768 + (2 * g + h) * AQK
                                ins = flip_of(bank[4 + g][0:AQK, h * S + t * P:h * S + (t + 1) * P], qk[:, a:a + AQK], ident)
                        ins.then_inc(ev("qk_flip"), 1)

                def attend(t):
                    pe.wait_ge(ev("qk_t"), 8 * (l + 1))
                    if t:
                        pe.wait_ge(ev("mla_y"), 2 * l + 1)
                    for h in range(AH):
                        ins = mm(bank[4 + h // 2][:, (h % 2) * S:(h % 2 + 1) * S],
                                 q_t[0:AQK, h * S + t * P:h * S + (t + 1) * P], k_t[0:AQK, h * S:(h + 1) * S], start=True, stop=True)
                    ins.then_inc(ev("logits"), 1)

                def weights(t):
                    pe.wait_ge(ev("prob"), 2 * l + t + 1)
                    for g in range(4):
                        for i in range(4):
                            ins = flip_of(bank[4 + g][:, i * P:(i + 1) * P], prob[:, (4 * g + i) * P:(4 * g + i + 1) * P], ident)
                        ins.then_inc(ev("prob_flip"), 1)

                def weigh(t):
                    o = bank[4]
                    pe.wait_ge(ev("prob_t"), 8 * l + 4 * t + 4)
                    for h in range(AH):
                        for s in range(NT):
                            ins = mm(o[:, h * AV:(h + 1) * AV], prob_t[:, (2 * h + s) * P:(2 * h + s + 1) * P],
                                     va[:, s * 512 + h * AV:s * 512 + (h + 1) * AV], start=s == 0, stop=s == 1)
                    ins.then_inc(ev("mla_o"), 1)

                def values():
                    pe.wait_ge(ev("conv3"), l + 1)
                    for t in range(NT):
                        for i in range(CT):
                            ins = flip_of(bank[6 + t][:, i * P:(i + 1) * P],
                                          conv_buf[0][:, i * S + t * P:i * S + (t + 1) * P], ident)
                    ins.then_inc(ev("c_flip"), 1)

                def rates():
                    pe.wait_ge(ev("dt_a"), l + 1)
                    for d in range(2):
                        for t in range(NT):
                            ins = flip_of(bank[5][0:SH, d * S + t * P:d * S + (t + 1) * P],
                                          dt_a[:, 32 * t + SH * d:32 * t + SH * (d + 1)], ident)
                    ins.then_inc(ev("dt_flip"), 1)
                    pe.wait_ge(ev("rows"), l + 1)
                    for i in range(4):
                        ins = flip_of(bank[4][:, i * SH:(i + 1) * SH], rows[0:SH, i * P:(i + 1) * P], ident[0:SH, 0:SH])
                    ins.then_inc(ev("rows_flip"), 1)

                def tokens_x():
                    pe.wait_ge(ev("xbc"), 3 * (l + 1))
                    pe.wait_ge(ev("row_cols"), l + 1)
                    pe.wait_ge(ev("conv_y"), l + 1)
                    for t in range(NT):
                        for i in range(XC):
                            ins = flip_of(bank[4 + 2 * t + i // 4][:, (i % 4) * P:(i % 4 + 1) * P],
                                          xbc[:, i * S + t * P:i * S + (t + 1) * P], ident)
                    ins.then_inc(ev("xs_flip"), 1)

                def cb_products():
                    pe.wait_ge(ev("xs"), l + 1)
                    for g in range(SG):
                        for s in range(NT):
                            b_t = xbc[:, (8 + g) * S + s * P:(8 + g) * S + (s + 1) * P]
                            ins = mm(bank[6 + g][:, s * S:(s + 1) * S], b_t, xbc[:, (10 + g) * S:(11 + g) * S], start=True, stop=True)
                    ins.then_inc(ev("cb"), 1)
                    pe.wait_ge(ev("pick"), 1)
                    pe.wait_ge(ev("rows_lo"), l + 1)
                    spread(0)
                    spread(1)

                def spread(h):
                    if h >= 2:
                        pe.wait_ge(ev("limited"), SH * l + h - 1)
                    mm(bank[4 + h % 2][:, :], pick[0:32 + SH, h:h + 1].to_broadcast([32 + SH, P]), rows_both,
                       start=True, stop=True).then_inc(ev("spread"), 1)

                def head(h):
                    if h == 0:
                        pe.wait_ge(ev("cb_out"), l + 1)
                    if h + 2 < SH:
                        spread(h + 2)
                    pe.wait_ge(ev("scores"), SH * l + h + 1)
                    if h == 8:
                        pe.wait_ge(ev("y_out"), 2 * l + 1)
                    e = expo[h % 3]
                    c = slice((h % 8) * SP_, (h % 8 + 1) * SP_)
                    x_head = [xs[:, t * D + h * SP_:t * D + (h + 1) * SP_] for t in range(NT)]
                    for t in range(NT):
                        mm(bank[6 + t][:, c], e[:, t * P:(t + 1) * P], x_head[0], start=True, stop=False)
                        ins = mm(bank[6 + t][:, c], e[:, 256 + t * P:256 + (t + 1) * P], x_head[1], start=False, stop=True)
                    ins.then_inc(ev("y_head"), 1)

                steps = {
                    "latents": latents, "keys_values": keys_values, "flip_q": lambda: flip_heads(0), "flip_k": lambda: flip_heads(1),
                    "attend_0": lambda: attend(0), "weights_0": lambda: weights(0),
                    "attend_1": lambda: attend(1), "weights_1": lambda: weights(1),
                    "weigh_0": lambda: weigh(0), "weigh_1": lambda: weigh(1),
                    "values": values, "rates": rates, "xs": tokens_x, "cb": cb_products,
                    **{f"head_{h}": lambda h=h: head(h) for h in range(SH)},
                }
                free = {2: ("u_part", 8 * l + 1), 3: ("kv_in", l + 1), 4: ("u_part", 8 * l + 3), 5: ("u_part", 8 * l + 4),
                        6: ("u_part", 8 * l + 5), 7: ("c_prod", l + 1), 8: ("u_part", 8 * l + 6)}
                for i, (c, u) in enumerate(IN_UNITS):
                    n = u0 + L_IN + i
                    if c is None:
                        mla_products(n)
                    else:
                        if i == 1:
                            pe.wait_ge(ev("xl_ready"), at("xl_ready", 8, l))
                        if u == 0 and c in free:
                            pe.wait_ge(ev(free[c][0]), free[c][1])
                        (unit_fm if c in FEATURE_MAJOR else unit_tm)(n, u, 2 * (c % 2), 448 if c == 0 else 512)
                    for name in STEPS.get(i, []):
                        if name in steps:
                            steps[name]()
                def flip_pair(p):
                    if p == 0:
                        pe.wait_ge(ev("side"), l + 1)
                        pe.wait_ge(ev("u_part"), 8 * (l + 1))
                    if p in (4, 6):
                        pe.wait_ge(ev("group"), 2 * l + (p - 2) // 2)
                    if p in (4, 5):
                        pe.wait_ge(ev("xl_ready"), at("xl_ready", 10 + MIX_BANK[p] + 1, l))
                    for jj in range(2):
                        for t in range(NT):
                            q = MIX_TILES[2 * p + jj]
                            ins = flip_of(bank[MIX_BANK[p]][:, jj * S + t * P:jj * S + (t + 1) * P],
                                          mix[:, t * 2 * D + q * P:t * 2 * D + (q + 1) * P], ident)
                    ins.then_inc(ev("flip"), 1)

                def between(c, u):
                    if c == 0 and u == 0:
                        pe.wait_ge(ev("xl_ready"), at("xl_ready", 14, l))
                    if c == 0 and u == 2:
                        flip_pair(6)
                        flip_pair(7)
                        pe.wait_ge(ev("xl_ready"), at("xl_ready", 16, l))
                    if c == 0 and u == 3:
                        pe.wait_ge(ev("xl_ready"), at("xl_ready", 18, l))

                for h in range(HEADS_BEFORE, SH):
                    head(h)
                    for p in FLIP_AFTER.get(h, []):
                        flip_pair(p)
                out_product(u0 + L_OUT, 4, between)
                late_norm(2, 18, l)
                ffn(u0 + L_FFN2, FFN_BLOCKS, blk + FFN_BLOCKS, at("xl_ready", 22, l))

            for l in range(LAYERS):
                layer(l)


def columns(w, c, width=512):
    k = w.shape[0]
    part = np.zeros((k, 512), w.dtype)
    part[:, :width] = w[:, c:c + width]
    return part.reshape(k // 512, 4, P, 512).transpose(0, 2, 1, 3).reshape(k // 512, P, UNIT)


def swiglu_units(gate, up, down):
    nb = gate.shape[1] // BLK

    def gate_up(b):
        c = slice(b * BLK, (b + 1) * BLK)
        return list(columns(np.concatenate([gate[:, c], up[:, c]], axis=1), 0))

    def rows(b):
        return [down[b * BLK:(b + 1) * BLK].reshape(2, P, D).transpose(1, 0, 2).reshape(P, UNIT)]

    units = gate_up(0)
    for b in range(1, nb):
        units += gate_up(b) + rows(b - 1)
    return units + rows(nb - 1)


def across(row):
    return np.broadcast_to(np.asarray(row).reshape(1, -1), (P, np.asarray(row).size))


def down_columns(v):
    return np.asarray(v).reshape(-1, P).T


def nope_rows(gain):
    out = np.ones((P, 1), np.float32)
    out[:NOPE, 0] = gain[:NOPE]
    return out


def table(spec, values):
    out = np.zeros((P, sum(w for _, w in spec)), np.float32)
    at = 0
    for name, width in spec:
        out[:, at:at + width] = values[name]
        at += width
    return out


def constants():
    p = np.arange(P)
    half = np.zeros((P, 2), np.float32)
    half[:64, 0] = half[64:, 1] = 0.125
    freq = 10000.0 ** (-np.arange(ROPE // 2, dtype=np.float32) / np.float32(ROPE // 2))
    return {
        "causal": np.concatenate([np.zeros((P, P)), np.where(p[:, None] >= p[None, :], 0.0, -BIG)], axis=1),
        "half_scale": half, "desc4": across(np.array([4, 3, 2, 1], np.float32)),
        "inv_freq": across(freq.astype(np.float32)),
    }


def array_constants():
    s, t = np.arange(P)[:, None], np.arange(P)[None, :]
    return np.concatenate([s == t, s <= t, s >= t], axis=1).astype(np.float32)


def level_masks():
    s, t = np.arange(P)[:, None], np.arange(P)[None, :]
    out = [s == t]
    for i in range(1, LEVELS + 1):
        w = 1 << (i - 1)
        out.append((s // (2 * w) == t // (2 * w)) & (s % (2 * w) < w) & (t % (2 * w) >= w))
    return np.stack(out, axis=1).astype(np.float32).reshape(P, -1)


def kernel(**inputs):
    import concourse.bacc as bacc
    from concourse.bass_utils import run_bass_kernel_spmd

    a = {k: np.asarray(v) for k, v in inputs.items()}
    units = []
    for c in IN1_TILES:
        units += list(columns(a["w_in"][0], c * 512))
    for c in range(2):
        units += list(columns(a["w_out"][0], c * 512))
    gate, up, down = a["w_gate"][0], a["w_up"][0], a["w_down"][0]
    units += swiglu_units(gate.transpose(1, 0, 2).reshape(D, NE * EF), up.transpose(1, 0, 2).reshape(D, NE * EF),
                          down.reshape(NE * EF, D))
    lp = []
    for l in range(LAYERS):
        units += swiglu_units(a["ffn1_w_gate_2"][l], a["ffn1_w_up_2"][l], a["ffn1_w_down_2"][l])
        w = a["w_in_2"][l]
        cols = layer_columns()
        in_units = [unit for c, width in cols for unit in columns(w, c, width)]
        uq = a["mla_w_uq_2"][l].reshape(2, P, AH * AQK).transpose(1, 0, 2).reshape(P, -1)
        in_units.insert(MLA_AT, np.concatenate([uq, a["mla_w_ukv_2"][l][:, :512]], axis=1))
        units += in_units
        for c in range(2):
            out_units = list(columns(a["w_out_2"][l], c * 512))
            units += out_units[2:] + out_units[:2]
        units += swiglu_units(a["ffn2_w_gate_2"][l], a["ffn2_w_up_2"][l], a["ffn2_w_down_2"][l])
        cw5, cw3 = a["ssd_conv_w_2"][l], a["conv_w_2"][l]
        lp.append(table(LAYER_PARAMS, {
            "ffn1_gain": down_columns(a["ffn1_norm_2"][l]), "mix_gain": down_columns(a["mix_norm_2"][l]),
            "ffn2_gain": down_columns(a["ffn2_norm_2"][l]),
            "conv5_w": cw5.reshape(5, XT, P).transpose(2, 1, 0).reshape(P, -1),
            "conv5_b": down_columns(a["ssd_conv_b_2"][l]),
            "dt_bias": across(a["ssd_dt_bias_2"][l]), "a_log": across(a["ssd_a_log_2"][l]),
            "d_skip": across(a["ssd_d_2"][l]), "ssd_gain": across(a["ssd_norm_2"][l]),
            "q_gain": down_columns(a["mla_q_norm_2"][l]), "kv_gain": down_columns(a["mla_kv_norm_2"][l]),
            "qh_rows": nope_rows(a["mla_q_head_norm_2"][l]), "kh_rows": nope_rows(a["mla_k_head_norm_2"][l]),
            "qh_rope": across(a["mla_q_head_norm_2"][l][NOPE:]), "kh_rope": across(a["mla_k_head_norm_2"][l][NOPE:]),
            "mla_gain": across(a["mla_out_norm_2"][l]),
            "conv3_w": cw3.reshape(3, CT, P).transpose(2, 1, 0).reshape(P, -1),
            "conv_gain": across(a["conv_out_norm_2"][l]),
        }))
    assert len(units) == N_UNITS
    small = np.concatenate([a["w_in"][0][:, 7 * 512:], a["w_group"][0], a["w_expert"][0]], axis=1)
    fox_bias = np.zeros((P, 1), np.float32)
    fox_bias[:FH, 0] = a["fox_f_bias"][0]
    prm = table(PARAMS, {
        **constants(), "attn_gain": down_columns(a["attn_norm"][0]), "ffn_gain": down_columns(a["ffn_norm"][0]),
        "lb_logits": a["hg_lb_logits"].reshape(2, HH, P).transpose(2, 0, 1).reshape(P, -1),
        "hg_gain": across(a["hg_norm"][0]), "fox_gain": across(a["fox_norm"][0]), "fox_bias": fox_bias,
        "router_bias": across(np.concatenate([a["b_group"][0], a["b_expert"][0]])),
        "small_w": small.reshape(KD, P, -1).transpose(1, 0, 2).reshape(P, -1),
    })
    arrays = {
        "stream": np.stack(units), "x_in": a["x"][0],
        "positions": np.ascontiguousarray(a["positions_2"].reshape(NT, P).T), "params": prm,
        "level_masks": level_masks(), "array_constants": array_constants(),
        "final_gain": a["final_norm"].reshape(1, D), "ukv": a["mla_w_ukv_2"][:, :, 512:], "layer_params": np.stack(lp),
    }
    nc = bacc.Bacc("TRN2", target_bir_lowering=False, num_devices=1)
    aps = [nc.dram_tensor(n, v.shape, mybir.dt.from_np(v.dtype), kind="ExternalInput").ap() for n, v in arrays.items()]
    out = nc.dram_tensor("out", (S, D), F32, kind="ExternalOutput").ap()
    two_blocks(nc, *aps, out)
    got = run_bass_kernel_spmd(nc, [arrays], core_ids=[0]).results[0]["out"]
    return got.reshape(1, S, D)


def layer_columns():
    xbc, dt, conv = SH * SP_, SH * SP_ + XT * P, SH * SP_ + XT * P + 448
    return ([(dt, 448)] + [(xbc + 512 * i, 512) for i in range(3)] + [(conv, 512), (conv + 1024, 512)]
            + [(conv + 512, 512)] + [(512 * i, 512) for i in range(2)])
```
